# Optimizing a Trainium2 kernel written in Bass

```python
import jax, jax.numpy as jnp
from jax import lax
import numpy as np

D_MODEL = 2048
BATCH = 1
SEQ = 256
DEPTH = 1

PLE_DIM = 256
EPS = 1e-6

N_HEADS_MLA = 16
Q_LORA = 512
KV_LORA = 512
QK_NOPE = 128
QK_ROPE = 64
V_DIM = 128
QK_DIM = QK_NOPE + QK_ROPE
ROPE_THETA = 10000.0
Q_BLOCK = 128

SSM_EXPAND = 2
D_INNER = SSM_EXPAND * D_MODEL
SSM_HEADDIM = 64
N_HEADS_SSM = D_INNER // SSM_HEADDIM
SSM_GROUPS = 8
HEADS_PER_GROUP = N_HEADS_SSM // SSM_GROUPS
D_STATE = 128
CONV_WIDTH = 4
CHUNK = 256
CONV_DIM = D_INNER + 2 * SSM_GROUPS * D_STATE

D_FF = ((8 * D_MODEL // 3 + 255) // 256) * 256

IN_SPLITS = (Q_LORA, KV_LORA, QK_ROPE, D_INNER, CONV_DIM, N_HEADS_SSM, D_MODEL, D_MODEL)
D_IN_PROJ = Q_LORA + KV_LORA + QK_ROPE + D_INNER + CONV_DIM + N_HEADS_SSM + 2 * D_MODEL

kernel_name = "hybrid_mla_ssd_gated_block"

def rms_norm(x, w):
    xf = x.astype(jnp.float32)
    y = xf * lax.rsqrt(jnp.mean(xf * xf, axis=-1, keepdims=True) + EPS)
    return (y * w.astype(jnp.float32)).astype(x.dtype)

def split_cols(t, sizes):
    outs, off = [], 0
    for s in sizes:
        outs.append(t[..., off:off + s])
        off += s
    return outs

def rotary_tables(positions, dim):
    inv_freq = ROPE_THETA ** (-jnp.arange(0, dim, 2, dtype=jnp.float32) / dim)
    ang = positions.astype(jnp.float32)[..., None] * inv_freq
    return jnp.cos(ang)[:, :, None, :], jnp.sin(ang)[:, :, None, :]

def apply_rope(x, cos, sin):
    xf = x.astype(jnp.float32)
    x1, x2 = jnp.split(xf, 2, axis=-1)
    out = jnp.concatenate([x1 * cos - x2 * sin, x2 * cos + x1 * sin], axis=-1)
    return out.astype(x.dtype)

def causal_block_attention(q, k, v):
    b, s, h, dk = q.shape
    nblk = s // Q_BLOCK
    scale = dk ** -0.5
    qb = jnp.moveaxis(q.reshape(b, nblk, Q_BLOCK, h, dk), 1, 0)
    key_idx = jnp.arange(s)

    def one_block(args):
        q_blk, blk = args
        sc = jnp.einsum('bqhd,bkhd->bhqk', q_blk, k, preferred_element_type=jnp.float32) * scale
        q_idx = blk * Q_BLOCK + jnp.arange(Q_BLOCK)
        mask = key_idx[None, :] <= q_idx[:, None]
        sc = jnp.where(mask[None, None], sc, -jnp.inf)
        prob = jax.nn.softmax(sc, axis=-1).astype(v.dtype)
        return jnp.einsum('bhqk,bkhd->bqhd', prob, v)

    o = lax.map(one_block, (qb, jnp.arange(nblk)))
    return jnp.moveaxis(o, 0, 1).reshape(b, s, h * v.shape[-1])

def mla_branch(c_q, c_kv, k_r, cos, sin, q_norm, w_uq, kv_norm, w_ukv):
    b, s, _ = c_q.shape
    q = (rms_norm(c_q, q_norm) @ w_uq).reshape(b, s, N_HEADS_MLA, QK_DIM)
    q_nope, q_pe = q[..., :QK_NOPE], apply_rope(q[..., QK_NOPE:], cos, sin)
    kv = (rms_norm(c_kv, kv_norm) @ w_ukv).reshape(b, s, N_HEADS_MLA, QK_NOPE + V_DIM)
    k_nope, v = kv[..., :QK_NOPE], kv[..., QK_NOPE:]
    k_pe = apply_rope(k_r[:, :, None, :], cos, sin)
    k = jnp.concatenate([k_nope, jnp.broadcast_to(k_pe, (b, s, N_HEADS_MLA, QK_ROPE))], axis=-1)
    q = jnp.concatenate([q_nope, q_pe], axis=-1)
    return causal_block_attention(q, k, v)

def causal_depthwise_conv(t, w, bias):
    out = lax.conv_general_dilated(
        t, w[:, None, :].astype(t.dtype), window_strides=(1,),
        padding=[(CONV_WIDTH - 1, 0)], dimension_numbers=('NWC', 'WIO', 'NWC'),
        feature_group_count=t.shape[-1])
    return out + bias

def ssd_chunked(x, dt, a, bm, cm):
    b, s, g, r, p = x.shape
    n = bm.shape[-1]
    nc = -(-s // CHUNK)
    pad = nc * CHUNK - s
    padw = lambda t: jnp.pad(t, [(0, 0), (0, pad)] + [(0, 0)] * (t.ndim - 2))
    xdt = padw(x * dt[..., None])
    da = padw(dt * a)
    bm, cm = padw(bm), padw(cm)
    chunks = lambda t: jnp.moveaxis(t.reshape((b, nc, CHUNK) + t.shape[2:]), 1, 0)
    causal = jnp.tril(jnp.ones((CHUNK, CHUNK), dtype=bool))[None, :, :, None, None]

    def step(state, inp):
        xc, ac, bc, cc = inp
        cum = jnp.cumsum(ac, axis=1)
        seg = cum[:, :, None] - cum[:, None, :]
        decay = jnp.exp(jnp.where(causal, seg, -jnp.inf))
        cb = jnp.einsum('bign,bjgn->bijg', cc, bc)
        y_diag = jnp.einsum('bijgr,bjgrp->bigrp', cb[..., None] * decay, xc)
        y_off = jnp.einsum('bign,bgrpn->bigrp', cc, state) * jnp.exp(cum)[..., None]
        last = cum[:, -1]
        w_end = jnp.exp(last[:, None] - cum)
        state = state * jnp.exp(last)[..., None, None] + jnp.einsum(
            'bjgn,bjgrp->bgrpn', bc, xc * w_end[..., None])
        return state, y_diag + y_off

    state0 = jnp.zeros((b, g, r, p, n), jnp.float32)
    _, ys = lax.scan(step, state0, (chunks(xdt), chunks(da), chunks(bm), chunks(cm)))
    ys = jnp.moveaxis(ys, 0, 1).reshape(b, nc * CHUNK, g, r, p)
    return ys[:, :s]

def mamba2_branch(z, xbc, dt_raw, conv_w, conv_b, dt_bias, a_log, d_skip, ssm_norm):
    b, s, _ = z.shape
    xbc = jax.nn.silu(causal_depthwise_conv(xbc, conv_w, conv_b))
    xs, bm, cm = split_cols(xbc, (D_INNER, SSM_GROUPS * D_STATE, SSM_GROUPS * D_STATE))
    xh = xs.reshape(b, s, SSM_GROUPS, HEADS_PER_GROUP, SSM_HEADDIM).astype(jnp.float32)
    dt = jax.nn.softplus(dt_raw.astype(jnp.float32) + dt_bias.astype(jnp.float32))
    dt = dt.reshape(b, s, SSM_GROUPS, HEADS_PER_GROUP)
    a = -jnp.exp(a_log.astype(jnp.float32)).reshape(SSM_GROUPS, HEADS_PER_GROUP)
    y = ssd_chunked(xh, dt, a,
                    bm.reshape(b, s, SSM_GROUPS, D_STATE).astype(jnp.float32),
                    cm.reshape(b, s, SSM_GROUPS, D_STATE).astype(jnp.float32))
    y = y + d_skip.astype(jnp.float32).reshape(SSM_GROUPS, HEADS_PER_GROUP)[..., None] * xh
    y = y.reshape(b, s, D_INNER).astype(z.dtype) * jax.nn.silu(z)
    y = rms_norm(y.reshape(b, s, SSM_GROUPS, D_INNER // SSM_GROUPS),
                 ssm_norm.reshape(SSM_GROUPS, D_INNER // SSM_GROUPS))
    return y.reshape(b, s, D_INNER)

def setup_inputs(seed: int = 0) -> dict:
    key = jax.random.key(seed)
    ks = jax.random.split(key, 32)
    f32 = jnp.float32
    nrm = lambda k, shape, fan_in: jax.random.normal(k, shape, f32) * fan_in ** -0.5
    gain = lambda k, dim: 1.0 + 0.02 * jax.random.normal(k, (DEPTH, dim), f32)
    dt0 = jnp.exp(jax.random.uniform(ks[12], (DEPTH, N_HEADS_SSM), f32)
                  * (np.log(0.1) - np.log(0.001)) + np.log(0.001))
    return {
        "x": jax.random.normal(ks[0], (BATCH, SEQ, D_MODEL), f32),
        "p": jax.random.normal(ks[1], (DEPTH, BATCH, SEQ, PLE_DIM), f32),
        "positions": jnp.broadcast_to(jnp.arange(SEQ, dtype=jnp.int32), (BATCH, SEQ)),
        "mix_norm_pre": gain(ks[2], D_MODEL),
        "mix_norm_post": gain(ks[3], D_MODEL),
        "w_in": nrm(ks[4], (DEPTH, D_MODEL, D_IN_PROJ), D_MODEL),
        "q_norm": gain(ks[5], Q_LORA),
        "w_uq": nrm(ks[6], (DEPTH, Q_LORA, N_HEADS_MLA * QK_DIM), Q_LORA),
        "kv_norm": gain(ks[7], KV_LORA),
        "w_ukv": nrm(ks[8], (DEPTH, KV_LORA, N_HEADS_MLA * (QK_NOPE + V_DIM)), KV_LORA),
        "conv_w": nrm(ks[9], (DEPTH, CONV_WIDTH, CONV_DIM), CONV_WIDTH),
        "conv_b": 0.01 * jax.random.normal(ks[10], (DEPTH, CONV_DIM), f32),
        "dt_bias": dt0 + jnp.log(-jnp.expm1(-dt0)),
        "a_log": jnp.log(jax.random.uniform(ks[11], (DEPTH, N_HEADS_SSM), f32, 1.0, 16.0)),
        "d_skip": 1.0 + 0.02 * jax.random.normal(ks[13], (DEPTH, N_HEADS_SSM), f32),
        "ssm_norm": gain(ks[14], D_INNER),
        "w_attn_o": nrm(ks[15], (DEPTH, N_HEADS_MLA * V_DIM, D_MODEL), N_HEADS_MLA * V_DIM),
        "w_ssm_o": nrm(ks[16], (DEPTH, D_INNER, D_MODEL), D_INNER),
        "w_out": nrm(ks[17], (DEPTH, D_MODEL, D_MODEL), D_MODEL),
        "ffn_norm_pre": gain(ks[18], D_MODEL),
        "ffn_norm_post": gain(ks[19], D_MODEL),
        "w_gate": nrm(ks[20], (DEPTH, D_MODEL, D_FF), D_MODEL),
        "w_up": nrm(ks[21], (DEPTH, D_MODEL, D_FF), D_MODEL),
        "w_down": nrm(ks[22], (DEPTH, D_FF, D_MODEL), D_FF),
        "ple_norm_pre": gain(ks[23], D_MODEL),
        "ple_norm_post": gain(ks[24], D_MODEL),
        "w_ple_gate": nrm(ks[25], (DEPTH, D_MODEL, D_MODEL), D_MODEL),
        "w_ple": nrm(ks[26], (DEPTH, PLE_DIM, D_MODEL), PLE_DIM),
    }

def reference(x, p, positions, mix_norm_pre, mix_norm_post, w_in, q_norm, w_uq, kv_norm, w_ukv,
              conv_w, conv_b, dt_bias, a_log, d_skip, ssm_norm, w_attn_o, w_ssm_o, w_out,
              ffn_norm_pre, ffn_norm_post, w_gate, w_up, w_down,
              ple_norm_pre, ple_norm_post, w_ple_gate, w_ple):
    cos, sin = rotary_tables(positions, QK_ROPE)
    h = x
    for i in range(DEPTH):
        u = rms_norm(h, mix_norm_pre[i])
        proj = u @ w_in[i]
        c_q, c_kv, k_r, z, xbc, dt_raw, g_attn, g_ssm = split_cols(proj, IN_SPLITS)
        attn = mla_branch(c_q, c_kv, k_r, cos, sin, q_norm[i], w_uq[i], kv_norm[i], w_ukv[i])
        ssm = mamba2_branch(z, xbc, dt_raw, conv_w[i], conv_b[i], dt_bias[i], a_log[i],
                            d_skip[i], ssm_norm[i])
        mixed = jax.nn.sigmoid(g_attn) * (attn @ w_attn_o[i]) + jax.nn.sigmoid(g_ssm) * (ssm @ w_ssm_o[i])
        h = h + rms_norm(mixed @ w_out[i], mix_norm_post[i])
        f = rms_norm(h, ffn_norm_pre[i])
        f = (jax.nn.silu(f @ w_gate[i]) * (f @ w_up[i])) @ w_down[i]
        h = h + rms_norm(f, ffn_norm_post[i])
        gate = jax.nn.sigmoid(rms_norm(h, ple_norm_pre[i]) @ w_ple_gate[i])
        e = (p[i].astype(h.dtype) @ w_ple[i]) * gate
        h = h + rms_norm(e, ple_norm_post[i])
    return h


_drawn_inputs = setup_inputs


def setup_inputs(seed=0):
    import zlib

    import numpy as np

    out = dict(_drawn_inputs(seed))
    spreads = {}
    factors = {'mix_norm_post': 4.035,
     'q_norm': 8.0,
     'kv_norm': 8.0,
     'conv_b': 5.687,
     'd_skip': 31.949,
     'ssm_norm': 18.556,
     'ffn_norm_pre': 3.862,
     'ffn_norm_post': 19.938,
     'ple_norm_pre': 34.093,
     'ple_norm_post': 25.619}
    for name, (base, spread) in spreads.items():
        noise = np.random.default_rng([zlib.crc32(name.encode()), seed]).standard_normal(out[name].shape)
        drawn = base * np.exp(spread * noise) if base else spread * noise
        out[name] = __import__('jax').numpy.asarray(drawn.astype(out[name].dtype))
    for name, factor in factors.items():
        out[name] = (out[name] * factor).astype(out[name].dtype)
    return out
```

```python
from contextlib import ExitStack

import numpy as np
import concourse.bass as bass
from concourse import mybir

F32 = mybir.dt.float32
F32R = mybir.dt.float32r
I32 = mybir.dt.int32
ALU = mybir.AluOpType
ACT = mybir.ActivationFunctionType

D_MODEL, SEQ, PLE_DIM, EPS = 2048, 256, 256, 1e-6
HEADS, Q_LORA, KV_LORA, NOPE, ROPE, VDIM = 16, 512, 512, 128, 64, 128
QK = NOPE + ROPE
SCALE = float(QK) ** -0.5
THETA = 10000.0
D_INNER, GROUPS, STATE, PDIM = 4096, 8, 128, 64
HEADS_SSM = D_INNER // PDIM
HPG = HEADS_SSM // GROUPS
CONV_DIM = D_INNER + 2 * GROUPS * STATE
D_FF = ((8 * D_MODEL // 3 + 255) // 256) * 256

C_Q = 0
C_KV = C_Q + Q_LORA
C_KR = C_KV + KV_LORA
C_Z = C_KR + ROPE
C_X = C_Z + D_INNER
C_B = C_X + D_INNER
C_DT = C_X + CONV_DIM
C_GA = C_DT + HEADS_SSM
C_GS = C_GA + D_MODEL

P = 128
KT = D_MODEL // P
NEG = -1.0e30
RING = 4
CHUNK = 1024

PHASES = {
    "kr": (4, 1),
    "ssm": (20, 8),
    "cq": (16, 1),
    "so": (12, 8),
    "at": (4, 8),
    "ao": (8, 8),
    "wo": (8, 4),
    "ff": (8, 22),
    "dn": (24, 4),
    "pl": (4, 1),
    "pg": (8, 4),
}
BASE = {}
_n = 0
for _k, (_c, _i) in PHASES.items():
    BASE[_k] = _n
    _n += _c * _i
DN_KT = [4] * 8 + [3] * 4
DN_AT = [sum(DN_KT[:i]) for i in range(12)]

V_MIXPRE, V_MIXPOST, V_FFPRE, V_FFPOST, V_PLPRE, V_PLPOST, V_QN, V_KVN = 0, 16, 32, 48, 64, 80, 96, 100
V_KEEP = 104
V_CB, V_SN, V_TAP = 104, 152, 184
V_ALL = 376
GP_N = 38


def num(phase, it, c):
    return it * PHASES[phase][0] + (BASE[phase] + c)


def build(nc, x, p_in, positions, mix_norm_pre, mix_norm_post, w_in, q_norm, w_uq, kv_norm, w_ukv,
          conv_w, conv_b, dt_bias, a_log, d_skip, ssm_norm, w_attn_o, w_ssm_o, w_out,
          ffn_norm_pre, ffn_norm_post, w_gate, w_up, w_down,
          ple_norm_pre, ple_norm_post, w_ple_gate, w_ple, cst_in, rope_in, out):
    V, S, T = nc.vector, nc.scalar, nc.tensor

    START = 16512
    CONST0 = START
    RAW0 = CONST0 + 8032
    HI0 = RAW0 + RING * CHUNK * 4
    LO0 = HI0 + RING * CHUNK * 4
    U0 = LO0 + RING * CHUNK * 4
    G0 = U0 + KT * 2048
    T0 = G0 + 44 * 2048
    H0 = T0 + 16384
    END = H0 + 16384
    assert END <= 229344

    def region(start, end):
        at = [start]

        def place(name, shape, dt=F32):
            size = int(np.prod(shape[1:])) * 4
            t = nc.alloc_sbuf_tensor_at(name, list(shape), dt, offset=at[0])
            at[0] += (size + 31) // 32 * 32
            assert at[0] <= end, (name, at[0], end)
            return t
        return place

    const = region(CONST0, RAW0)
    cst = const("cst", [P, 384])
    ident, tri, ones, tri_ones = cst[:, 0:128], cst[:, 128:256], cst[:, 256:384], cst[:, 128:384]
    pv = const("pv", [P, V_KEEP])
    gp_all = const("gp_all", [P, GROUPS, GP_N])
    gp_main = const("gp_main", [P, 30])
    gp_side = const("gp_side", [P, 8])
    dt_tok = const("dt_tok", [P, 2, HEADS_SSM])
    cum_tok = const("cum_tok", [P, 2, HEADS_SSM])
    cum_g = const("cum_g", [P, 2, HPG])
    dt_g = const("dt_g", [P, 2, HPG])
    keep = const("keep", [P, 3, SEQ])
    kr, r_q, r_kv = keep[:, 0, :], keep[:, 1, :], keep[:, 2, :]
    sqc = keep[:, 1:3, :]
    rkv_tok = const("rkv_tok", [P, 2])
    pad = const("pad", [P, 1])

    def at(name, shape, offset, dt=F32):
        return nc.alloc_sbuf_tensor_at(name, list(shape), dt, offset=offset)

    raw = at("raw", [P, RING, CHUNK], RAW0)
    whi = at("whi", [P, RING, CHUNK], HI0, F32R)
    wlo = at("wlo", [P, RING, CHUNK], LO0, F32R)
    u = at("u", [P, KT, 2, SEQ], U0, F32R)
    g = at("g", [P, 44, 2, SEQ], G0, F32R)
    m = at("m", [P, KT, SEQ], T0)
    h = at("h", [P, KT, SEQ], H0)

    first = region(G0, G0 + 32 * 2048)
    x_tok = first("x_tok", [P, 2, D_MODEL])
    xn_tok = first("xn_tok", [P, 2, D_MODEL])
    sq_tok = first("sq_tok", [P, D_MODEL])
    rows = first("rows", [P, 4, P])
    pv_all = first("pv_all", [P, V_ALL])
    st0 = first("st0", [P, 8])
    prep = region(G0 + 32 * 2048, G0 + 36 * 2048)
    dtb = prep("dtb", [P, HEADS_SSM])
    alog = prep("alog", [P, HEADS_SSM])
    dsk = prep("dsk", [P, HEADS_SSM])
    d_xb, d_e, d_r, d_s, d_s2, d_q, da = (prep(n, [P, 2, HEADS_SSM])
                                          for n in ("d_xb", "d_e", "d_r", "d_s", "d_s2", "d_q", "da"))
    cumt = prep("cumt", [HEADS_SSM, SEQ])
    ssm = region(T0, END)
    acc_q = ssm("acc_q", [P, 2, SEQ])
    rs = ssm("rs", [P, 3, SEQ])
    xs = ssm("xs", [P, 6, SEQ])
    z = ssm("z", [P, 4, SEQ])
    cumb = ssm("cumb", [P, HPG, SEQ])
    cbm = ssm("cbm", [P, 384])
    xdt = ssm("xdt", [P, 2, 4, 192])
    e = at("e", [P, 4, 384], G0 + 32 * 2048)
    sq = at("sq", [P, 4, SEQ], G0 + 32 * 2048)
    yb = at("yb", [P, 2, SEQ], G0 + 35 * 2048)
    c = at("c", [P, 8, 2, SEQ], G0 + 36 * 2048, F32R)
    late = region(H0, END)
    sg = late("sg", [P, 2, SEQ])
    prod = late("prod", [P, 2, SEQ])
    cos, sin, kpe, a_ang, a_k, a_s, a_c = (late(n, [P, SEQ])
                                           for n in ("cos", "sin", "kpe", "a_ang", "a_k", "a_s", "a_c"))
    pos_i = late("pos_i", [P, SEQ], I32)
    rope_c = late("rope_c", [P, 513])
    mask_a, rotm, invf = rope_c[:, 0:384], rope_c[:, 384:512], rope_c[:, 512:513]
    attn = region(G0 + 16 * 2048, G0 + 32 * 2048)
    qn = attn("qn", [P, 2, SEQ])
    qp = attn("qp", [P, SEQ])
    qr = attn("qr", [P, 2, SEQ])
    rt = attn("rt", [P, 2, SEQ])
    kn = attn("kn", [P, 2, SEQ])
    vt = attn("vt", [P, 2, 2, VDIM])
    sc = attn("sc", [P, 2, 384])
    pt = attn("pt", [P, 2, 384])
    mx, nm, ls, rl = (attn(n, [P, 2, 2]) for n in ("mx", "nm", "ls", "rl"))
    x_tok2 = at("x_tok2", [P, 2, D_MODEL], G0)
    work = region(G0 + 8 * 2048, G0 + 16 * 2048)
    sq_n = work("sq_n", [P, 2, 2, SEQ])
    acc_n = work("acc_n", [P, 2, SEQ])
    bt = work("bt", [P, 2, SEQ])
    fg = at("fg", [P, 2, SEQ], T0)
    fu = at("fu", [P, 2, SEQ], T0 + 2048)
    sq_d = at("sq_d", [P, 2, SEQ], U0)
    acc_d = at("acc_d", [P, 2, SEQ], U0 + 2048)
    p_tok = at("p_tok", [P, 2, PLE_DIM], U0 + 12 * 2048)
    pc = at("pc", [P, 2, 2, SEQ], U0 + 14 * 2048, F32R)
    ee = at("ee", [P, KT, SEQ], G0)
    ga = at("ga", [P, 2, SEQ], G0 + 16 * 2048)
    ot = at("ot", [P, 2, D_MODEL], G0 + 20 * 2048)

    psum = nc.alloc_psum_tensor("acc", [P, 8, 512], F32)

    def bank(b):
        return psum[:, b, :]

    cum_dram = nc.dram_tensor("cum_scratch", [HEADS_SSM, SEQ], F32, kind="Internal").ap()

    CREDIT = {"sg_so": 1, "so_ev": 1, "sg_ao": 1, "ao_ev": 1, "wo_sq": 2, "ffg_ev": 1, "ffu_ev": 1,
              "dn_sq": 2, "pg_ev": 2, "wo_acc": 1, "dn_acc": 1, "pg_acc": 1, "ssm_lo": 1}
    ACCQ = (0, 1, 3, 4, 6)
    names = {}

    def sem(name):
        if name not in names:
            names[name] = nc.alloc_semaphore(name)
        return names[name]

    raw_in = [sem(f"raw_in{i}") for i in range(RING)]

    w_in4 = w_in.rearrange("(q t p) n -> q p t n", t=4, p=P)
    w_uq2 = w_uq.rearrange("(q t p) n -> q p t n", t=2, p=P)
    w_ukv4 = w_ukv.rearrange("(t p) n -> p t n", p=P)
    w_so4 = w_ssm_o.rearrange("(q t p) n -> q p t n", t=4, p=P)
    w_ao4 = w_attn_o.rearrange("(q t p) n -> q p t n", t=4, p=P)
    w_wo4 = w_out.rearrange("(q t p) n -> q p t n", t=4, p=P)
    w_g4 = w_gate.rearrange("(q t p) n -> q p t n", t=4, p=P)
    w_u4 = w_up.rearrange("(q t p) n -> q p t n", t=4, p=P)
    w_dn = w_down.rearrange("(t p) n -> p t n", p=P)
    w_pg4 = w_ple_gate.rearrange("(q t p) n -> q p t n", t=4, p=P)
    w_pl2 = w_ple.rearrange("(t p) n -> p t n", p=P)
    D_IN = w_in.shape[1]

    def source(phase, it, c):
        ds = bass.ds
        if phase == "kr":
            return [w_in4[c][:, :, first:first + 64] for first in (C_KR, C_KR, C_DT)]
        if phase == "ssm":
            q, k = divmod(c, 4)
            if q == 0:
                return [w_in4[k][:, :, ds(it * STATE + first, STATE)] for first in (C_B, C_B + GROUPS * STATE)]
            first_col = {1: C_X, 2: C_X + 256, 3: C_Z, 4: C_Z + 256}[q]
            return [w_in4[k][:, :, ds(it * 512 + first_col, 256)]]
        if phase == "cq":
            q, k = divmod(c, 4)
            return [w_in4[k][:, :, 256 * q:256 * q + 256]]
        if phase == "so":
            if c < 4:
                return [w_in4[c][:, :, ds(it * 256 + C_GS, 256)]]
            return [w_so4[c - 4][:, :, ds(it * 256, 256)]]
        if phase == "at":
            if c < 2:
                return [w_uq2[c][:, :, ds(it * (2 * QK) + first, n)]
                        for first, n in ((0, NOPE), (QK, NOPE), (NOPE, ROPE), (QK + NOPE, ROPE))]
            return [w_ukv4[:, :, ds(it * 512 + 256 * (c - 2), 256)]]
        if phase == "ao":
            if c < 4:
                return [w_in4[c][:, :, ds(it * 256 + C_GA, 256)]]
            return [w_ao4[c - 4][:, :, ds(it * 256, 256)]]
        if phase == "wo":
            q, k = divmod(c, 4)
            return [w_wo4[k][:, :, ds(it * 512 + 256 * q, 256)]]
        if phase == "ff":
            return [(w_g4 if c < 4 else w_u4)[c % 4][:, :, ds(it * 256, 256)]]
        if phase == "dn":
            q, k = divmod(c, 12)
            return [w_dn[:, DN_AT[k]:DN_AT[k] + DN_KT[k], ds(it * 512 + 256 * q, 256)]]
        if phase == "pl":
            return [w_pl2[:, :, 512 * c:512 * c + 512]]
        q, k = divmod(c, 4)
        return [w_pg4[k][:, :, ds(it * 512 + 256 * q, 256)]]

    FIRST_COLUMN = {"so": (4,), "at": (0, 2), "ao": (4,), "wo": (0,), "ff": (0, 4), "dn": (0,), "pg": (0,)}

    def width(phase, c):
        if phase == "kr":
            return 4 * 192
        if phase == "at" and c < 2:
            return 2 * 2 * QK
        if phase == "dn":
            return DN_KT[c % 12] * 256
        return CHUNK

    def loads(phase, it, c):
        n = it * (PHASES[phase][0] // RING) + (BASE[phase] // RING + c // RING + 3)
        if phase == "kr":
            return n
        if phase == "ssm":
            return n + (it + 1)
        n = n + GROUPS
        if c % RING < 2 and phase != "cq" and phase != "so":
            return n + 3 * (it + 1) if phase == "at" else n + 3 * PHASES["at"][1]
        return n

    ctx = ExitStack()
    block = ctx.enter_context(nc.Block())

    @block.sync
    def _(sp):
        x_view = x.rearrange("(b p) d -> b p d", p=P)
        for b in range(2):
            sp.dma_start(x_tok[:, b, :], x_view[b]).then_inc(sem(f"x_in{b}"), 16)
        sp.dma_start(cst[:, :], cst_in).then_inc(sem("cst_in"), 16)
        for phase, (per, its) in PHASES.items():
            def load(it, c):
                slot = c % RING
                w = width(phase, c)
                parts = source(phase, it, c)
                dst = raw[:, slot, 0:w].rearrange("p (t n) -> p t n", t=parts[0].shape[1])
                if phase != "kr":
                    sp.wait_ge(sem("lo_ready"), num(phase, it, c) - RING + 1)
                    if c in FIRST_COLUMN.get(phase, ()):
                        sp.sem_inc(sem("slot_free"), 1)
                o = 0
                for src in parts:
                    sp.dma_start(dst[:, :, o:o + src.shape[2]], src).then_inc(raw_in[slot], 16)
                    o += src.shape[2]
            if its == 1:
                for c_ in range(per):
                    load(0, c_)
            else:
                with sp.Fori(0, its) as it:
                    for c_ in range(per):
                        load(it, c_)
        out_view = out.rearrange("(b p) d -> p b d", p=P)
        for q in range(4):
            sp.wait_ge(sem("ot_ready"), 2 * q + 2)
            sp.dma_start(out_view[:, :, 512 * q:512 * q + 512],
                         ot[:, :, 512 * q:512 * q + 512]).then_inc(sem("out_done"), 16)
        sp.wait_ge(sem("out_done"), 64)

    @block.gpsimd
    def _(pool):
        vec = [(mix_norm_pre, 16, 0), (mix_norm_post, 16, 16), (ffn_norm_pre, 16, 32), (ffn_norm_post, 16, 48),
               (ple_norm_pre, 16, 64), (ple_norm_post, 16, 80), (q_norm, 4, 96), (kv_norm, 4, 100)]
        for v, n, at_row in vec:
            pool.dma_start(rows[at_row:at_row + n, 0, :], v.rearrange("(t p) -> t p", p=P)) \
                .then_inc(sem("rows_in"), 16)
        pool.dma_start(rows[0:48, 1, :], conv_b.rearrange("(t p) -> t p", p=P)).then_inc(sem("rows_in"), 16)
        pool.dma_start(rows[48:80, 1, :], ssm_norm.rearrange("(t p) -> t p", p=P)).then_inc(sem("rows_in"), 16)
        for i in range(2):
            pool.dma_start(rows[0:96, 2 + i, :],
                           conv_w[2 * i:2 * i + 2, :].rearrange("a (t p) -> (a t) p", p=P)) \
                .then_inc(sem("rows_in"), 16)
        for v, dst in ((dt_bias, dtb), (a_log, alog), (d_skip, dsk)):
            pool.dma_start(dst[:, :], v.partition_broadcast(P)).then_inc(sem("heads_in"), 16)
        pool.wait_ge(sem("cumt_ev"), 1)
        pool.dma_start(cum_dram, cumt[:, :]).then_inc(sem("cum_out"), 16)
        pool.wait_ge(sem("cum_out"), 16)

        def load_cum(gi):
            pool.dma_start(cumb[:, :, :].rearrange("p h s -> p (h s)"),
                           cum_dram[bass.ds(gi * HPG, HPG), :].rearrange("h s -> (h s)").partition_broadcast(P)) \
                .then_inc(sem("cumb_in"), 16)
        load_cum(0)
        with pool.Fori(1, GROUPS) as gi:
            pool.wait_ge(sem("seg"), gi * (2 * HPG))
            load_cum(gi)
        pool.wait_ge(sem("ssm_lo"), GROUPS + CREDIT["ssm_lo"])
        pool.dma_start(pos_i[:, :], positions.partition_broadcast(P)).then_inc(sem("pos_in"), 16)
        pool.dma_start(rope_c[:, :], rope_in).then_inc(sem("rope_in"), 16)
        pool.wait_ge(sem("chunk_done"), BASE["wo"])
        for b in range(2):
            pool.dma_start(x_tok2[:, b, :], x.rearrange("(b p) d -> b p d", p=P)[b]) \
                .then_inc(sem("x_in2"), 16)
        pool.wait_ge(sem("chunk_done"), BASE["dn"])
        pool.dma_start(p_tok[:, :, :], p_in.rearrange("(b p) d -> p b d", p=P)).then_inc(sem("p_in"), 16)

    @block.tensor
    def _(pe):
        for name, n in CREDIT.items():
            pe.sem_inc(sem(name), n)

        def mm3(o, wh, wl, xh, xl, start, stop):
            T.matmul(o, wh, xh, start=start, stop=False, skip_group_check=True)
            T.matmul(o, wh, xl, start=False, stop=False, skip_group_check=True)
            return T.matmul(o, wl, xh, start=False, stop=stop, skip_group_check=True)

        def begin(phase, it, c):
            pe.wait_ge(sem("lo_ready"), num(phase, it, c) + 1)

        def ring(c, n):
            slot = c % RING
            return (whi[:, slot, :].rearrange("p (t n) -> p t n", n=n),
                    wlo[:, slot, :].rearrange("p (t n) -> p t n", n=n))

        def chunk(phase, it, c, banks, src, kts, start, stop, cols=256):
            begin(phase, it, c)
            wh, wl = ring(c, cols)
            for i, b in enumerate(banks):
                for j, kt in enumerate(kts):
                    last = mm3(bank(b)[:, 0:SEQ], wh[:, j, i * P:i * P + P], wl[:, j, i * P:i * P + P],
                               src[:, kt, 0, :], src[:, kt, 1, :],
                               start and j == 0, stop and j == len(kts) - 1)
            last.then_inc(sem("chunk_done"), 1)

        def group(phase, it, c0, banks, src, k0=0, n=4, after=None):
            for i in range(n):
                chunk(phase, it, c0 + i, banks, src, range(k0 + 4 * i, k0 + 4 * i + 4), i == 0, i == n - 1)
                if after:
                    after(i)

        pe.wait_ge(sem("cst_in"), 16)
        pe.wait_ge(sem("rows_in"), 12 * 16)
        at_col = 0
        for i, n in enumerate((V_KEEP, 80, 96, 96)):
            last = T.transpose(bank(7)[:, at_col:at_col + n], rows[0:n, i, :], cst[0:n, 0:n])
            at_col += n
        last.then_inc(sem("pv_mm"), 1)
        for b in range(8):
            if b == 0:
                pe.wait_ge(sem("xn_ready"), 2)
            if b == 7:
                pe.wait_ge(sem("pv_ev"), 1)
            for k in range(2):
                for blk in range(2):
                    kt = 2 * b + k
                    last = T.transpose(bank(b)[:, k * SEQ + blk * P:k * SEQ + blk * P + P],
                                       xn_tok[:, blk, kt * P:kt * P + P], ident)
            last.then_inc(sem("xt_mm"), 1)

        for c_ in range(4):
            begin("kr", 0, c_)
            pe.wait_ge(sem("u_lo"), max(6, 4 * c_ + 4))
            wh, wl = ((w[:, c_, 0:4 * 192].rearrange("p (t n) -> p t n", n=192)) for w in (whi, wlo))
            for j in range(4):
                kt = 4 * c_ + j
                st, sp_ = kt == 0, kt == KT - 1
                mm3(bank(0)[:, 0:SEQ], wh[:, j, 0:P], wl[:, j, 0:P], u[:, kt, 0, :], u[:, kt, 1, :], st, sp_)
                for blk in range(2):
                    o, t = bank(1 + blk)[:, 0:64], slice(blk * P, blk * P + P)
                    T.matmul(o, u[:, kt, 0, t], wh[:, j, P:192], start=st, stop=False, skip_group_check=True)
                    T.matmul(o, u[:, kt, 0, t], wl[:, j, P:192], start=False, stop=False, skip_group_check=True)
                    last = T.matmul(o, u[:, kt, 1, t], wh[:, j, P:192], start=False, stop=sp_,
                                    skip_group_check=True)
            last.then_inc(sem("chunk_done"), 1)

        def cum_sums():
            pe.wait_ge(sem("da_ready"), 1)
            T.matmul(bank(6)[:, 0:64], tri, da[:, 0, :], start=True, stop=True)
            T.matmul(bank(6)[:, 64:128], ones, da[:, 0, :], start=True, stop=False)
            T.matmul(bank(6)[:, 64:128], tri, da[:, 1, :], start=False, stop=True).then_inc(sem("cum_mm"), 1)
            T.matmul(bank(7)[0:64, 0:SEQ], da[:, 0, :], tri_ones, start=True, stop=False)
            T.matmul(bank(7)[0:64, P:SEQ], da[:, 1, :], tri, start=False, stop=True).then_inc(sem("cum_mm"), 1)

        def ssd_step(it, c_):
            if c_ == 0:
                pe.wait_ge(sem("xs_act"), it)
                T.matmul(bank(6)[:, 0:256], xs[:, 4, 0:128], xs[:, 5, :], start=True, stop=True)
                T.matmul(bank(6)[:, 256:384], xs[:, 4, 128:256], xs[:, 5, 128:256], start=True, stop=True) \
                    .then_inc(sem("cb_mm"), 1)
            if c_ in (0, 3):
                blk = c_ // 3
                if blk:
                    pe.wait_ge(sem("cbm_ev"), it)
                for t in range(4):
                    last = T.transpose(bank(7 - blk)[:, t * P:t * P + P], xs[:, t, blk * P:blk * P + P], ident)
                last.then_inc(sem("xtr_mm"), 1)
            if c_ in (5, 7, 9, 11):
                p = (c_ - 5) // 2
                b = 7 - p % 2
                if p == 0:
                    pe.wait_ge(sem("xdt_ready"), it * 2)
                if p >= 2:
                    pe.wait_ge(sem("y_skip"), it * 4 - 4 + p - 1)
                pe.wait_ge(sem("masked"), it * 8 - 8 + 2 * p + 2)
                ea, eb = e[:, 2 * p % 4, :], e[:, (2 * p + 1) % 4, :]
                T.matmul(bank(b)[:, 0:256], xdt[:, 0, p, 0:128], ea[:, 0:256], start=True, stop=False,
                         skip_group_check=True)
                T.matmul(bank(b)[:, 128:256], xdt[:, 1, p, 0:128], ea[:, 256:384], start=False, stop=False,
                         skip_group_check=True)
                T.matmul(bank(b)[:, 128:256], xdt[:, 1, p, 64:192], eb[:, 256:384], start=False, stop=False,
                         skip_group_check=True)
                T.matmul(bank(b)[:, 0:256], xdt[:, 0, p, 64:192], eb[:, 0:256], start=False, stop=True,
                             skip_group_check=True).then_inc(sem("y_mm"), 1)
            if c_ == 14:
                pe.wait_ge(sem("sq_ready"), it)
                for t in range(4):
                    last = T.matmul(bank(7)[:, 0:256], ones, sq[:, t, :], start=t == 0, stop=t == 3)
                last.then_inc(sem("ss_mm"), 1)

        def ssm_group(it):
            head = isinstance(it, int)
            for c_ in range(20):
                q, k = divmod(c_, 4)
                banks = ((4, 5), (0, 1), (2, 3), (0, 1), (2, 3))[q]
                if k == 0:
                    if q == 0 and not head:
                        pe.wait_ge(sem("conv_done"), it * 6 - 4)
                    if q == 1 and head:
                        pe.wait_ge(sem("kr_ev"), 1)
                        pe.wait_ge(sem("dt_xb"), 2)
                    if q in (1, 2) and not head:
                        pe.wait_ge(sem("z_act"), it)
                    if q == 3:
                        pe.wait_ge(sem("conv_done"), it * 6 + 4)
                    if q == 4:
                        pe.wait_ge(sem("conv_done"), it * 6 + 6)
                chunk("ssm", it, c_, banks, u, range(4 * k, 4 * k + 4), k == 0, k == 3)
                if head and c_ == 11:
                    cum_sums()
                if not head:
                    ssd_step(it, c_)

        ssm_group(0)
        with pe.Fori(1, GROUPS) as it:
            ssm_group(it)

        for c_ in range(16):
            q, k = divmod(c_, 4)
            banks = ((4, 5), (0, 1), (2, 3), (4, 5))[q]
            if k == 0 and q == 0:
                pe.wait_ge(sem("conv_done"), GROUPS * 6 - 4)
            if k == 0 and q in (1, 2):
                pe.wait_ge(sem("z_act"), GROUPS)
            if k == 0 and q == 3:
                pe.wait_ge(sem("c_lo"), 2)
            chunk("cq", 0, c_, banks, u, range(4 * k, 4 * k + 4), k == 0, k == 3)
            ssd_step(GROUPS, c_)

        def so_iter(it, after=None):
            pe.wait_ge(sem("sg_so"), it + CREDIT["sg_so"])
            group("so", it, 0, (0, 1), u, after=after)
            pe.wait_ge(sem("so_ev"), it + CREDIT["so_ev"])
            if isinstance(it, int):
                pe.wait_ge(sem("ssm_lo"), GROUPS + CREDIT["ssm_lo"])
            group("so", it, 4, (2, 3), g, n=8)

        def norms_qkv(i):
            if i == 3:
                pe.wait_ge(sem("accq"), ACCQ[4])
                for k in range(2):
                    pe.wait_ge(sem("ms"), GROUPS)
                    T.matmul(bank(6 + k)[:, 0:SEQ], ones, acc_q[:, k, :], start=True, stop=True) \
                        .then_inc(sem("ssqkv_mm"), 1)

        pe.wait_ge(sem("c_lo"), 6)
        so_iter(0, norms_qkv)
        pe.wait_ge(sem("rope_tab"), 1)
        pe.wait_ge(sem("c_lo"), 8)
        T.matmul(bank(4)[:, 0:SEQ], rotm, kr, start=True, stop=True).then_inc(sem("krot_mm"), 1)
        pe.wait_ge(sem("rkv_ready"), 1)
        for blk in range(2):
            last = T.transpose(bank(5)[:, blk * P:blk * P + P], r_kv[:, blk * P:blk * P + P], ident)
        last.then_inc(sem("rkvt_mm"), 1)
        with pe.Fori(1, 8) as it:
            so_iter(it)

        def attn_before(it):
            pe.wait_ge(sem("qp_ev"), it)
            T.matmul(bank(6)[:, 0:SEQ], rotm, qp[:, :], start=True, stop=True).then_inc(sem("rot_mm"), 1)

        def attn_scores(it):
            pe.wait_ge(sem("kv_ev"), it * 2)
            pe.wait_ge(sem("rope_done"), it * 2)
            if not isinstance(it, int) or it > 1:
                pe.wait_ge(sem("o_lo"), it - 1)
            for hd in range(2):
                for q, o, n in ((0, 0, 128), (1, 128, 256)):
                    t = slice(q * P, q * P + P)
                    T.matmul(bank(4 + hd)[:, o:o + n], qn[:, hd, t], kn[:, hd, 0:n], start=True, stop=False)
                    last = T.matmul(bank(4 + hd)[:, o:o + n], qr[:, hd, t], kpe[:, 0:n], start=False, stop=True)
                last.then_inc(sem("scores_mm"), 1)

        def attn_values(it):
            for hd in range(2):
                pe.wait_ge(sem("pn"), it * 2 - 1 + hd)
                for j in range(3):
                    last = T.transpose(bank(6 + hd)[:, j * P:j * P + P], sc[:, hd, j * P:j * P + P], ident)
                last.then_inc(sem("pt_mm"), 1)
            for hd in range(2):
                pe.wait_ge(sem("pt_ev"), it * 2 - 1 + hd)
                T.matmul(bank(4 + hd)[:, 0:SEQ], vt[:, hd, 0, :], pt[:, hd, 0:256], start=True, stop=False,
                         skip_group_check=True)
                T.matmul(bank(4 + hd)[:, P:SEQ], vt[:, hd, 1, :], pt[:, hd, 256:384], start=False, stop=True,
                             skip_group_check=True).then_inc(sem("av_mm"), 1)

        def attn_main(it, c_):
            begin("at", it, c_)
            if c_ < 2:
                if c_ == 0:
                    if isinstance(it, int) and it == 0:
                        pe.wait_ge(sem("sg_so"), 8 + CREDIT["sg_so"])
                        pe.wait_ge(sem("so_ev"), 8 + CREDIT["so_ev"])
                        pe.wait_ge(sem("rkvt_ev"), 1)
                    else:
                        pe.wait_ge(sem("q_ev"), it)
                wh, wl = ((w[:, c_ % RING, 0:768].rearrange("p (t n) -> p t n", n=2 * QK)) for w in (whi, wlo))
                for j in range(2):
                    kt = 2 * c_ + j
                    st, sp_ = kt == 0, kt == 3
                    x2 = (c[:, kt, 0, :], c[:, kt, 1, :])
                    for hd in range(2):
                        o = slice(hd * NOPE, hd * NOPE + NOPE)
                        mm3(bank(0)[:, hd * SEQ:hd * SEQ + SEQ], wh[:, j, o], wl[:, j, o], *x2,
                            st and hd == 0, sp_ and hd == 1)
                    o = slice(2 * NOPE, 2 * QK)
                    last = mm3(bank(2)[:, 0:SEQ], wh[:, j, o], wl[:, j, o], *x2, st, sp_)
            else:
                b = 3 if c_ == 2 else 1
                if not (isinstance(it, int) and it == 0):
                    pe.wait_ge(sem("kv_ev"), it * 2 - 1 + (c_ - 2))
                wh, wl = ring(c_, 256)
                for j in range(4):
                    kt = 4 + j
                    st, sp_ = j == 0, j == 3
                    mm3(bank(b)[:, 0:SEQ], wh[:, j, 0:NOPE], wl[:, j, 0:NOPE], c[:, kt, 0, :], c[:, kt, 1, :],
                        st, False)
                    for blk in range(2):
                        o, t = bank(b)[:, SEQ + blk * P:SEQ + blk * P + P], slice(blk * P, blk * P + P)
                        for n_, (a_, w_) in enumerate(((0, wh), (0, wl), (1, wh))):
                            last = T.matmul(o, c[:, kt, a_, t], w_[:, j, NOPE:NOPE + VDIM], start=False,
                                            stop=sp_ and n_ == 2 and blk == 1, skip_group_check=True)
            last.then_inc(sem("chunk_done"), 1)

        def attn_iter(it):
            attn_before(it)
            attn_main(it, 0)
            attn_main(it, 1)
            attn_scores(it)
            attn_main(it, 2)
            attn_main(it, 3)
            attn_values(it)

        for c_ in range(4):
            attn_main(0, c_)
        attn_iter(1)
        with pe.Fori(2, 8) as it:
            attn_iter(it)

        def ao_iter(it, after=None):
            if isinstance(it, int):
                pe.wait_ge(sem("q_ev"), 8)
                pe.wait_ge(sem("kv_ev"), 16)
            pe.wait_ge(sem("sg_ao"), it + CREDIT["sg_ao"])
            group("ao", it, 0, (0, 1), u, after=after)
            pe.wait_ge(sem("ao_ev"), it + CREDIT["ao_ev"])

            for i in range(4):
                if isinstance(it, int) and i == 0:
                    pe.wait_ge(sem("o_lo"), 7)
                if isinstance(it, int) and i == 3:
                    pe.wait_ge(sem("o_lo"), 8)
                chunk("ao", it, 4 + i, (2, 3), g, range(4 * i, 4 * i + 4), i == 0, i == 3)

        attn_before(8)

        def last_pair(i):
            if i == 1:
                attn_scores(8)
            if i == 3:
                attn_values(8)
        ao_iter(0, last_pair)
        with pe.Fori(1, 8) as it:
            ao_iter(it)

        def two_groups(phase, it, src, k0, free, after=None, gate=None):
            for c_ in range(8):
                q, k = divmod(c_, 4)
                if k == 0:
                    pe.wait_ge(sem(free), it * 2 + (q - 1) + CREDIT[free])
                if gate:
                    gate(k)
                chunk(phase, it, c_, ((0, 1), (2, 3))[q], src, range(k0 + 4 * k, k0 + 4 * k + 4), k == 0, k == 3)
                if after:
                    after(c_)

        def mixed_ready(k):
            pe.wait_ge(sem("ao_lo"), 2 * k + 2)

        def x_again(c_):
            if c_ in (0, 1, 4, 5):
                i = (0, 1, 4, 5).index(c_)
                if i == 0:
                    pe.wait_ge(sem("x_in2"), 32)
                    pe.wait_ge(sem("o_lo"), 8)
                for b in (4 + 2 * (i % 2), 5 + 2 * (i % 2)):
                    kt = 4 * i + 2 * (b % 2)
                    if i >= 2:
                        pe.wait_ge(sem("h_ev"), 2 * (i - 2) + b % 2 + 1)
                    for k in range(2):
                        for blk in range(2):
                            last = T.transpose(bank(b)[:, k * SEQ + blk * P:k * SEQ + blk * P + P],
                                               x_tok2[:, blk, (kt + k) * P:(kt + k) * P + P], ident)
                    last.then_inc(sem("ht_mm"), 1)

        with pe.Fori(0, 3) as it:
            two_groups("wo", it, g, 16, "wo_sq", gate=mixed_ready)
        two_groups("wo", 3, g, 16, "wo_sq", after=x_again)

        def ss_total(acc, done, n, b):
            pe.wait_ge(sem(done), n + CREDIT[done])
            for k in range(2):
                last = T.matmul(bank(b)[:, 0:SEQ], ones, acc[:, k, :], start=k == 0, stop=k == 1)
            last.then_inc(sem("tot_mm"), 1)

        def norm_pairs(step):
            def after(i):
                if i < 4:
                    for j in (2 * i, 2 * i + 1):
                        pe.wait_ge(sem("hsq"), 8 * step + j + 1)
                        for k in range(2):
                            last = T.matmul(bank(6)[:, 0:SEQ], ones, sq_n[:, j % 2, k, :],
                                            start=j == 0 and k == 0, stop=j == 7 and k == 1,
                                            skip_group_check=True)
                        last.then_inc(sem("hss_mm"), 1)
            return after

        pe.wait_ge(sem("h_ev"), 8)
        ss_total(acc_n, "wo_acc", 8, 7)

        def ff_iter(it, after=None, ready=False):
            pe.wait_ge(sem("ffg_ev"), it + CREDIT["ffg_ev"])
            for i in range(4):
                if ready:
                    pe.wait_ge(sem("u_lo"), 16 + 4 * i + 4)
                chunk("ff", it, i, (0, 1), u, range(4 * i, 4 * i + 4), i == 0, i == 3)
                if after:
                    after(i)
            pe.wait_ge(sem("ffu_ev"), it + CREDIT["ffu_ev"])
            group("ff", it, 4, (2, 3), u)
        ff_iter(0, norm_pairs(0), True)
        with pe.Fori(1, 22) as it:
            ff_iter(it)

        with pe.Fori(0, 4) as it:
            for c_ in range(24):
                q, k = divmod(c_, 12)
                if k == 0:
                    pe.wait_ge(sem("dn_sq"), it * 2 + (q - 1) + CREDIT["dn_sq"])
                    pe.wait_ge(sem("ffu_ev"), 22 + CREDIT["ffu_ev"])
                    pe.wait_ge(sem("ff_lo"), 20)
                if k == 10:
                    pe.wait_ge(sem("ff_lo"), 21)
                if k == 11:
                    pe.wait_ge(sem("ff_lo"), 22)
                chunk("dn", it, c_, ((0, 1), (2, 3))[q], g, range(DN_AT[k], DN_AT[k] + DN_KT[k]), k == 0, k == 11)

        pe.wait_ge(sem("p_in"), 16)
        for k in range(2):
            for blk in range(2):
                last = T.transpose(bank(4)[:, k * SEQ + blk * P:k * SEQ + blk * P + P],
                                   p_tok[:, blk, k * P:k * P + P], ident)
        last.then_inc(sem("pt8_mm"), 1)
        pe.wait_ge(sem("pc_lo"), 1)
        for c_ in range(4):
            if c_:
                pe.wait_ge(sem("ee_ev"), c_)
            chunk("pl", 0, c_, (4, 5, 6, 7), pc, range(2), True, True, cols=512)
            if c_ == 0:
                ss_total(acc_d, "dn_acc", 8, 0)
        pe.wait_ge(sem("ee_ev"), 4)
        pe.wait_ge(sem("tot_ms"), 2)

        def second_ready(k):
            pe.wait_ge(sem("u_lo"), 32 + 4 * k + 4)
        two_groups("pg", 0, u, 0, "pg_ev", after=norm_pairs(1), gate=second_ready)
        with pe.Fori(1, 4) as it:
            two_groups("pg", it, u, 0, "pg_ev")
        ss_total(acc_n, "pg_acc", 8, 4)
        for j in range(8):
            pe.wait_ge(sem("h_new"), 16 + j + 1)
            if j == 0:
                pe.wait_ge(sem("tot_ms"), 3)
            for blk in range(2):
                for k in range(2):
                    last = T.transpose(bank(j)[:, blk * SEQ + k * P:blk * SEQ + k * P + P],
                                       h[:, 2 * j + k, blk * P:blk * P + P], ident)
            last.then_inc(sem("ot_mm"), 1)

    @block.scalar
    def _(act):
        def split(phase, it, c):
            slot, w = c % RING, width(phase, c)
            act.wait_ge(raw_in[slot], loads(phase, it, c) * 16)
            if phase != "kr":
                act.wait_ge(sem("chunk_done"), num(phase, it, c) - RING + 1)
            S.activation(whi[:, slot, 0:w], raw[:, slot, 0:w], ACT.Copy).then_inc(sem("hi_ready"), 1)

        def group_end(phase, it, c_last):
            act.wait_ge(sem("chunk_done"), num(phase, it, c_last) + 1)

        def rstd(src, tmp, name, n):
            act.wait_ge(sem(name + "_ms"), n)
            S.activation(tmp, src, ACT.Ln).then_inc(sem(name + "_ln"), 1)
            act.wait_ge(sem(name + "_ln"), n)
            S.activation(tmp, tmp, ACT.Exp, scale=-0.5).then_inc(sem(name + "_r0"), 1)

        for b in range(2):
            act.wait_ge(sem(f"x_in{b}"), 16)
            S.activation(sq_tok[:, :], x_tok[:, b, :], ACT.Square, accum_out=st0[:, b:b + 1]) \
                .then_inc(sem("x_ssq"), 1)
            if b == 0:
                act.wait_ge(sem("x_ssq"), 1)
        rstd(st0[:, 2:4], st0[:, 4:6], "x", 1)
        act.wait_ge(sem("heads_in"), 48)
        S.activation(alog[:, :], alog[:, :], ACT.Exp).then_inc(sem("a_exp"), 1)
        act.wait_ge(sem("pv_ev"), 1)
        for b in range(8):
            act.wait_ge(sem("xt_mm"), b + 1)
            for k in range(2):
                kt = 2 * b + k
                S.activation(u[:, kt, 0, :], bank(b)[:, k * SEQ:k * SEQ + SEQ], ACT.Identity,
                                 scale=pv_all[:, V_MIXPRE + kt:V_MIXPRE + kt + 1]).then_inc(sem("u_hi"), 1)
            if b in (1, 3, 5, 6):
                split("kr", 0, (1, 3, 5, 6).index(b))
        group_end("kr", 0, 3)
        S.activation(kr, bank(0)[:, 0:SEQ], ACT.Copy).then_inc(sem("kr_ev"), 1)

        def conv_first(it, tiles, banks):
            for t, b in zip(tiles, banks):
                S.activation(xs[:, t, :], bank(b)[:, 0:SEQ], ACT.Identity,
                                 scale=gp_main[:, 18 + t:19 + t], bias=gp_main[:, 24 + t:25 + t]) \
                                     .then_inc(sem("conv_acc"), 1)

        def ssm_main(it, c_):
            head = isinstance(it, int)
            if c_ == 6:
                group_end("ssm", it, 3)
                act.wait_ge(sem("gpm"), it + 1)
                if not head:
                    act.wait_ge(sem("cb_mm"), it)
                conv_first(it, (4, 5), (4, 5))
            if c_ in (10, 14):
                i = (c_ - 10) // 4
                group_end("ssm", it, 7 + 4 * i)
                if not head:
                    act.wait_ge(sem("y_skip"), it * 4 + (2 * i - 2))
                conv_first(it, (2 * i, 2 * i + 1), (2 * i, 2 * i + 1))
            if c_ == 19:
                act.wait_ge(sem("conv_done"), it * 6 + 6)
                S.activation(xs[:, :, :], xs[:, :, :], ACT.Silu).then_inc(sem("xs_act"), 1)

        def ssm_side(it, c_):
            if c_ == 2:
                group_end("ssm", it - 1, 19)
                act.wait_ge(sem("ssm_lo"), it - 1 + CREDIT["ssm_lo"])
                S.activation(z[:, :, :], psum[:, 0:4, 0:SEQ], ACT.Silu).then_inc(sem("z_act"), 1)
            if c_ in (5, 6, 9, 11):
                p = (5, 6, 9, 11).index(c_)
                for hd in (2 * p, 2 * p + 1):
                    act.wait_ge(sem("seg"), it * 16 - 16 + 2 * hd + 2)
                    S.activation(e[:, hd % 4, :], e[:, hd % 4, :], ACT.Exp).then_inc(sem("decay"), 1)
            if c_ == 14:
                act.wait_ge(sem("yz"), it * 4)
                S.activation(sq[:, :, :], z[:, :, :], ACT.Square).then_inc(sem("sq_ready"), 1)
            if c_ == 18:
                act.wait_ge(sem("ms"), it)
                S.activation(rs[:, 1, :], rs[:, 0, :], ACT.Ln).then_inc(sem("ln"), 1)
                act.wait_ge(sem("ln"), it)
                S.activation(rs[:, 1, :], rs[:, 1, :], ACT.Exp, scale=-0.5).then_inc(sem("r0"), 1)
                act.wait_ge(sem("yn"), it * 4)
                S.activation(g[:, bass.ds(it * 4 - 4, 4), 0, :], z[:, :, :], ACT.Copy).then_inc(sem("ssm_hi"), 1)

        for c_ in range(20):
            split("ssm", 0, c_)
            if c_ == 2:
                act.wait_ge(sem("dt_xb"), 2)
                S.activation(d_e[:, :, :], d_xb[:, :, :], ACT.Abs).then_inc(sem("dt_abs"), 1)
                act.wait_ge(sem("dt_abs"), 1)
                S.activation(d_e[:, :, :], d_e[:, :, :], ACT.Exp, scale=-1.0).then_inc(sem("dt_exp"), 1)
            if c_ == 15:
                act.wait_ge(sem("cum_mm"), 2)
                S.activation(cumt[:, :], bank(7)[0:64, 0:SEQ], ACT.Copy).then_inc(sem("cumt_ev"), 1)
            ssm_main(0, c_)
        with act.Fori(1, GROUPS) as it:
            for c_ in range(20):
                split("ssm", it, c_)
                ssm_side(it, c_)
                ssm_main(it, c_)

        def split_c(q):
            group_end("cq", 0, 4 * q + 3)
            b = (4, 0, 2, 4)[q]
            for i in range(2):
                t = 2 * q + i
                col = (V_QN if t < 4 else V_KVN) + t % 4
                S.activation(c[:, t, 0, :], bank(b + i)[:, 0:SEQ], ACT.Identity, scale=pv[:, col:col + 1]) \
                    .then_inc(sem("c_hi"), 1)
            if q:
                act.wait_ge(sem("accq"), ACCQ[q])
            S.activation(sqc, psum[:, b:b + 2, 0:SEQ], ACT.Square).then_inc(sem("c_sq"), 1)

        for c_ in range(20):
            split(*(("cq", 0, c_) if c_ < 16 else ("so", 0, c_ - 16)))
            ssm_side(GROUPS, c_)
            if c_ in (6, 10, 14, 19):
                split_c((6, 10, 14, 19).index(c_))

        def so_gate(it):
            group_end("so", it, 3)
            act.wait_ge(sem("so_ev"), it + CREDIT["so_ev"])
            S.activation(sg[:, :, :], psum[:, 0:2, 0:SEQ], ACT.Sigmoid).then_inc(sem("sg_so"), 1)

        for c_ in range(4, 12):
            split("so", 0, c_)
            if c_ == 5:
                for k, r in ((0, r_q), (1, r_kv)):
                    act.wait_ge(sem("qkv_ms"), k + 1)
                    S.activation(r, rs[:, k, :], ACT.Ln).then_inc(sem("qkv_ln"), 1)
                for k, r in ((0, r_q), (1, r_kv)):
                    act.wait_ge(sem("qkv_ln"), k + 1)
                    S.activation(r, r, ACT.Exp, scale=-0.5).then_inc(sem("qkv_r0"), 1)
            if c_ == 6:
                act.wait_ge(sem("ssm_lo"), GROUPS + CREDIT["ssm_lo"])
                so_gate(0)
            if c_ == 9:
                act.wait_ge(sem("angles"), 2)
                S.activation(sin[:, :], a_s[:, :], ACT.Sin).then_inc(sem("rope_sin"), 1)
                S.activation(cos[:, :], a_c[:, :], ACT.Sin).then_inc(sem("rope_tab"), 1)
        with act.Fori(1, 8) as it:
            for c_ in range(12):
                split("so", it, c_)
                if c_ == 6:
                    so_gate(it)

        def attn_side(it, c_):
            if c_ == 0 and not (isinstance(it, int) and it < 2):
                act.wait_ge(sem("av_mm"), it * 2 - 2)
                S.activation(g[:, bass.ds(it * 2 - 4, 2), 0, :], psum[:, 4:6, 0:SEQ], ACT.Copy) \
                    .then_inc(sem("o_hi"), 1)
            if c_ == 2 and not (isinstance(it, int) and it > 8):
                for hd in range(2):
                    for q, o, n in ((0, 0, 128), (1, 128, 256)):
                        act.wait_ge(sem("smax"), it * 2 - 1 + hd)
                        S.activation(sc[:, hd, o:o + n], sc[:, hd, o:o + n], ACT.Exp,
                                         bias=nm[:, hd, q:q + 1], scale=SCALE,
                                         accum_out=ls[:, hd, q:q + 1]).then_inc(sem("pexp"), 1)
            if c_ == 3 and not (isinstance(it, int) and it > 8):
                for hd in range(2):
                    act.wait_ge(sem("pt_mm"), it * 2 - 1 + hd)
                    S.activation(pt[:, hd, :], bank(6 + hd)[:, 0:384], ACT.Copy).then_inc(sem("pt_ev"), 1)

        for c_ in range(4):
            split("at", 0, c_)
        for c_ in range(4):
            split("at", 1, c_)
            attn_side(1, c_)
        with act.Fori(2, 8) as it:
            for c_ in range(4):
                split("at", it, c_)
                attn_side(it, c_)

        def ao_gate(it):
            group_end("ao", it, 3)
            act.wait_ge(sem("ao_ev"), it + CREDIT["ao_ev"])
            S.activation(sg[:, :, :], psum[:, 0:2, 0:SEQ], ACT.Sigmoid).then_inc(sem("sg_ao"), 1)

        def ao_hi(it):
            act.wait_ge(sem("mixed"), it)
            S.activation(g[:, bass.ds(it * 2 + 14, 2), 0, :], prod[:, :, :], ACT.Copy).then_inc(sem("ao_hi"), 1)

        for c_ in range(8):
            split("ao", 0, c_)
            if c_ < 4:
                attn_side(8, c_)
            if c_ == 4:
                attn_side(9, 0)
            if c_ == 6:
                ao_gate(0)
        with act.Fori(1, 8) as it:
            for c_ in range(8):
                split("ao", it, c_)
                if c_ == 3:
                    ao_hi(it)
                if c_ == 6:
                    ao_gate(it)

        def sums_out(phase, k, last_chunk, src_banks, dst, sq_t, tile):
            group_end(phase, *last_chunk)
            S.activation(m[:, bass.ds(tile, 2), :], psum[:, src_banks:src_banks + 2, 0:SEQ], ACT.Copy) \
                .then_inc(sem(phase + "_cp"), 1)
            act.wait_ge(sem(phase + "_acc"), k + CREDIT[phase + "_acc"])
            S.activation(sq_t, psum[:, src_banks:src_banks + 2, 0:SEQ], ACT.Square) \
                .then_inc(sem(phase + "_sq"), 1)

        def wo_side(it, c_):
            if c_ == 6:
                sums_out("wo", it * 2, (it, 3), 0, m, sq_n[:, 0, :, :], it * 4)
            if c_ == 2 and not (isinstance(it, int) and it == 0):
                sums_out("wo", it * 2 - 1, (it - 1, 7), 2, m, sq_n[:, 0, :, :], it * 4 - 2)

        def h_copy(n):
            act.wait_ge(sem("ht_mm"), n + 1)
            b = (4, 5, 6, 7)[n % 4]
            S.activation(h[:, 2 * n:2 * n + 2, :], bank(b)[:, :], ACT.Copy).then_inc(sem("h_ev"), 1)

        for c_ in range(8):
            split("wo", 0, c_)
            if c_ == 3:
                ao_hi(8)
            wo_side(0, c_)
        with act.Fori(1, 4) as it:
            for c_ in range(8):
                split("wo", it, c_)
                wo_side(it, c_)
        for c_ in range(4):
            split("ff", 0, c_)
            wo_side(4, c_) if c_ == 2 else None
            if c_ == 0:
                for n in range(4):
                    h_copy(n)
            if c_ == 1:
                for n in range(4, 8):
                    h_copy(n)

        def residual(step, w, extra=None):
            for j in range(8):
                if extra:
                    extra(j)
                act.wait_ge(sem("h_new"), 8 * step + j + 1)
                for k in range(2):
                    kt = 2 * j + k
                    S.activation(u[:, kt, 0, :], h[:, kt, :], ACT.Identity, scale=pv[:, w + kt:w + kt + 1]) \
                        .then_inc(sem("u_hi"), 1)
                if 8 * step + j >= 2:
                    act.wait_ge(sem("hss_mm"), 8 * step + j - 1)
                S.activation(sq_n[:, j % 2, :, :], h[:, 2 * j:2 * j + 2, :], ACT.Square).then_inc(sem("hsq"), 1)

        rstd(keep[:, 0, :], keep[:, 1, :], "tot", 1)
        residual(0, V_FFPRE)

        def ff_side(it, c_):
            if c_ == 3 and not (isinstance(it, int) and it == 0):
                act.wait_ge(sem("ff_prod"), it)
                S.activation(g[:, bass.ds(it * 2 - 2, 2), 0, :], fu[:, :, :], ACT.Copy).then_inc(sem("ff_hi"), 1)
            if c_ == 6:
                act.wait_ge(sem("ffg_ev"), it + 1 + CREDIT["ffg_ev"])
                S.activation(fg[:, :, :], fg[:, :, :], ACT.Silu).then_inc(sem("ff_act"), 1)

        for c_ in range(4, 8):
            split("ff", 0, c_)
            if c_ == 5:
                rstd(keep[:, 0, :], keep[:, 1, :], "hn", 1)
            ff_side(0, c_)
        with act.Fori(1, 22) as it:
            for c_ in range(8):
                split("ff", it, c_)
                ff_side(it, c_)

        def dn_side(it, c_):
            if c_ == 14:
                sums_out("dn", it * 2, (it, 11), 0, m, sq_d[:, :, :], it * 4)
            if c_ == 2 and not (isinstance(it, int) and it == 0):
                sums_out("dn", it * 2 - 1, (it - 1, 23), 2, m, sq_d[:, :, :], it * 4 - 2)

        for c_ in range(24):
            split("dn", 0, c_)
            if c_ == 3:
                ff_side(22, 3)
            dn_side(0, c_)
        with act.Fori(1, 4) as it:
            for c_ in range(24):
                split("dn", it, c_)
                dn_side(it, c_)

        for c_ in range(4):
            split("pl", 0, c_)
            if c_ == 2:
                dn_side(4, 2)
        act.wait_ge(sem("pt8_mm"), 1)
        S.activation(pc[:, :, 0, :], bank(4)[:, :].rearrange("p (k s) -> p k s", k=2), ACT.Copy) \
            .then_inc(sem("pc_hi"), 1)

        def ee_out(n):
            act.wait_ge(sem("chunk_done"), BASE["pl"] + n + 1)
            S.activation(ee[:, 4 * n:4 * n + 4, :], psum[:, 4:8, 0:SEQ], ACT.Copy).then_inc(sem("ee_ev"), 1)

        def between(j):
            if j < 3:
                ee_out(j + 1)
            if j % 2 == 0:
                split("pg", 0, j // 2)
            if j == 6:
                act.wait_ge(sem("chunk_done"), BASE["pg"])
        ee_out(0)
        rstd(keep[:, 0, :], keep[:, 1, :], "tot", 2)
        residual(1, V_PLPRE, between)

        def pg_side(k, last_chunk, b, c_, tile):
            if c_ == 0:
                act.wait_ge(sem("pg_ev"), k + 1 + CREDIT["pg_ev"])
                S.activation(ga[:, :, :], ga[:, :, :], ACT.Sigmoid).then_inc(sem("pg_act"), 1)
            else:
                act.wait_ge(sem("pg_e"), k + 1)
                act.wait_ge(sem("pg_acc"), k + CREDIT["pg_acc"])
                S.activation(sq_n[:, 0, :, :], ee[:, bass.ds(tile, 2), :], ACT.Square).then_inc(sem("pg_sq"), 1)

        def pg_iter(it, c_):
            if c_ in (6, 7):
                pg_side(it * 2, (it, 3), 0, c_ - 6, it * 4)
            if c_ in (2, 3) and not (isinstance(it, int) and it == 0):
                pg_side(it * 2 - 1, (it - 1, 7), 2, c_ - 2, it * 4 - 2)

        for c_ in range(4, 8):
            split("pg", 0, c_)
            if c_ == 5:
                rstd(keep[:, 0, :], keep[:, 1, :], "hn", 2)
            pg_iter(0, c_)
        with act.Fori(1, 4) as it:
            for c_ in range(8):
                split("pg", it, c_)
                pg_iter(it, c_)
        pg_iter(4, 2)
        pg_iter(4, 3)
        rstd(keep[:, 0, :], keep[:, 1, :], "tot", 3)
        for j in range(8):
            act.wait_ge(sem("ot_mm"), j + 1)
            S.activation(ot[:, :, 2 * j * P:2 * j * P + 2 * P],
                             bank(j)[:, :].rearrange("p (b n) -> p b n", b=2), ACT.Copy) \
                                 .then_inc(sem("ot_ready"), 1)

    @block.vector
    def _(dve):
        def split(phase, it, c):
            slot, w = c % RING, width(phase, c)
            dve.wait_ge(sem("hi_ready"), num(phase, it, c) + 1)
            V.tensor_tensor(wlo[:, slot, 0:w], raw[:, slot, 0:w], whi[:, slot, 0:w].bitcast(F32), ALU.subtract) \
                .then_inc(sem("lo_ready"), 1)

        def group_end(phase, it, c_last):
            dve.wait_ge(sem("chunk_done"), num(phase, it, c_last) + 1)

        def both(r):
            return r.unsqueeze(1).to_broadcast([P, 2, SEQ])

        steps = [0]

        def link(ins):
            steps[0] += 1
            ins.then_inc(sem("dve_step"), 1)
            dve.wait_ge(sem("dve_step"), steps[0])

        def newton(ms, r0, tmp, final, dst=None):
            link(V.tensor_tensor(tmp, r0, r0, ALU.mult))
            link(V.scalar_tensor_tensor(tmp, tmp, -0.5, ms, ALU.mult, ALU.mult))
            ins = V.scalar_tensor_tensor(tmp if dst is None else dst, tmp, 1.5, r0, ALU.add, ALU.mult)
            if final:
                ins.then_inc(sem(final), 1)
            else:
                link(ins)

        dve.wait_ge(sem("pv_mm"), 1)
        V.tensor_copy(pv_all[:, :], bank(7)[:, 0:V_ALL]).then_inc(sem("pv_ev"), 1)
        dve.wait_ge(sem("pv_ev"), 1)
        V.tensor_copy(pv[:, :], pv_all[:, 0:V_KEEP]).then_inc(sem("pv_kept"), 1)
        dve.wait_ge(sem("x_ssq"), 2)
        link(V.memset(xdt[:, :, :, 64:128], 0.0))
        V.tensor_scalar(st0[:, 2:4], st0[:, 0:2], 1.0 / D_MODEL, EPS, ALU.mult, ALU.add).then_inc(sem("x_ms"), 1)
        taps = pv_all[:, V_TAP:V_ALL].rearrange("p (a n) -> p a n", a=4)
        gp_taps = gp_all[:, :, 0:24].rearrange("p g (a t) -> p a g t", t=6)
        V.tensor_copy(gp_taps[:, :, :, 0:4], taps[:, :, 0:32].rearrange("p a (g t) -> p a g t", t=4))
        for i in range(2):
            V.tensor_copy(gp_taps[:, :, :, 4 + i], taps[:, :, 32 + 8 * i:40 + 8 * i])
        V.tensor_copy(gp_all[:, :, 24:28], pv_all[:, V_CB:V_CB + 32].rearrange("p (g t) -> p g t", t=4))
        for i in range(2):
            V.tensor_copy(gp_all[:, :, 28 + i], pv_all[:, V_CB + 32 + 8 * i:V_CB + 40 + 8 * i])
        V.tensor_copy(gp_all[:, :, 30:34], pv_all[:, V_SN:V_SN + 32].rearrange("p (g t) -> p g t", t=4))
        dve.wait_ge(sem("heads_in"), 48)
        for i in range(2):
            half = slice(64 * i, 64 * i + 64)
            last = V.tensor_copy(gp_all[half, :, 34:38],
                                 dsk[half, :].rearrange("p (g t i) -> p g t i", t=4, i=2)[:, :, :, i])
            if i == 0:
                link(last)
        last.then_inc(sem("gp_all"), 1)
        dve.wait_ge(sem("gp_all"), 1)
        dve.wait_ge(sem("x_r0"), 1)
        newton(st0[:, 2:4], st0[:, 4:6], st0[:, 6:8], None)
        for b in range(2):
            V.tensor_scalar(xn_tok[:, b, :], x_tok[:, b, :], st0[:, 6 + b:7 + b], None, ALU.mult) \
                .then_inc(sem("xn_ready"), 1)
        for b in range(8):
            dve.wait_ge(sem("u_hi"), 2 * b + 2)
            for k in range(2):
                kt = 2 * b + k
                V.scalar_tensor_tensor(u[:, kt, 1, :], bank(b)[:, k * SEQ:k * SEQ + SEQ],
                                           pv_all[:, V_MIXPRE + kt:V_MIXPRE + kt + 1],
                                           u[:, kt, 0, :].bitcast(F32), ALU.mult, ALU.subtract) \
                                               .then_inc(sem("u_lo"), 1)
            if b in (2, 4, 6, 7):
                split("kr", 0, (2, 4, 6, 7).index(b))

        def prepare_dt():
            group_end("kr", 0, 3)
            for blk in range(2):
                V.tensor_tensor(d_xb[:, blk, :], bank(1 + blk)[:, 0:64], dtb[:, :], ALU.add) \
                    .then_inc(sem("dt_xb"), 1)

        def softplus():
            dve.wait_ge(sem("dt_exp"), 1)
            link(V.tensor_scalar(d_r[:, :, :], d_e[:, :, :], 2.0, None, ALU.add))
            link(V.reciprocal(d_r[:, :, :], d_r[:, :, :]))
            link(V.tensor_tensor(d_s[:, :, :], d_e[:, :, :], d_r[:, :, :], ALU.mult))
            link(V.tensor_tensor(d_s2[:, :, :], d_s[:, :, :], d_s[:, :, :], ALU.mult))
            link(V.tensor_scalar(d_q[:, :, :], d_s2[:, :, :], 2.0 / 15, None, ALU.mult))
            for k in (13, 11, 9, 7, 5, 3):
                link(V.scalar_tensor_tensor(d_q[:, :, :], d_q[:, :, :], 2.0 / k, d_s2[:, :, :], ALU.add, ALU.mult))
            link(V.scalar_tensor_tensor(d_q[:, :, :], d_q[:, :, :], 2.0, d_s[:, :, :], ALU.add, ALU.mult))
            link(V.scalar_tensor_tensor(dt_tok[:, :, :], d_xb[:, :, :], 0.0, d_q[:, :, :], ALU.max, ALU.add))
            dve.wait_ge(sem("a_exp"), 1)
            V.scalar_tensor_tensor(da[:, :, :], dt_tok[:, :, :], -1.0,
                                       alog[:, :].unsqueeze(1).to_broadcast([P, 2, HEADS_SSM]),
                                       ALU.mult, ALU.mult).then_inc(sem("da_ready"), 1)

        def conv_rest(it, pair, tiles, banks):
            for k, a in enumerate((2, 1, 0)):
                for i, (t, b) in enumerate(zip(tiles, banks)):
                    if k == 0:
                        dve.wait_ge(sem("conv_acc"), it * 6 + (2 * pair + i + 1))
                    else:
                        dve.wait_ge(sem("conv_tap"), it * 12 + (4 * pair + 2 * (k - 1) + i + 1))
                    sh = 3 - a
                    ins = V.scalar_tensor_tensor(xs[:, t, sh:SEQ], bank(b)[:, 0:SEQ - sh],
                                                 gp_main[:, 6 * a + t:6 * a + t + 1], xs[:, t, sh:SEQ],
                                                 ALU.mult, ALU.add)
                    ins.then_inc(sem("conv_done" if k == 2 else "conv_tap"), 1)

        def ssm_main(it, c_):
            if c_ == 0:
                if not isinstance(it, int):
                    dve.wait_ge(sem("conv_acc"), it * 6)
                V.tensor_copy(gp_main[:, :], gp_all[:, bass.ds(it, 1), 0:30].rearrange("p a n -> p (a n)")) \
                    .then_inc(sem("gpm"), 1)
                dve.wait_ge(sem("gpm"), it + 1)
            if c_ == 7:
                conv_rest(it, 0, (4, 5), (4, 5))
            if c_ == 11:
                conv_rest(it, 1, (0, 1), (0, 1))
            if c_ == 15:
                conv_rest(it, 2, (2, 3), (2, 3))

        def decays(it, p):
            for hd in (2 * p, 2 * p + 1):
                if hd >= 4:
                    dve.wait_ge(sem("y_mm"), it * 4 - 4 + (hd - 4) // 2 + 1)
                for blk, o, n in ((0, 0, 256), (1, 256, 128)):
                    V.tensor_scalar(e[:, hd % 4, o:o + n], cumb[:, hd, SEQ - n:SEQ], cum_g[:, blk, hd:hd + 1],
                                        0.0, ALU.subtract, ALU.min).then_inc(sem("seg"), 1)

        def mask_scores(it, p):
            for hd in (2 * p, 2 * p + 1):
                dve.wait_ge(sem("decay"), it * 8 - 8 + hd + 1)
                V.tensor_tensor(e[:, hd % 4, :], e[:, hd % 4, :], cbm[:, :], ALU.mult).then_inc(sem("masked"), 1)

        def x_dt(it, blk):
            dve.wait_ge(sem("xtr_mm"), it * 2 - 1 + blk)
            V.tensor_tensor(xdt[:, blk, :, :].rearrange("p q (a n) -> p q a n", a=3)[:, :, 0:3:2, :],
                                bank(7 - blk)[:, :].rearrange("p (q a n) -> p q a n", q=4, a=2),
                                dt_g[:, blk, :].rearrange("p (q a) -> p q a", a=2).unsqueeze(3)
                                .to_broadcast([P, 4, 2, PDIM]), ALU.mult).then_inc(sem("xdt_ready"), 1)

        def y_gate(it, p):
            dve.wait_ge(sem("y_mm"), it * 4 - 3 + p)
            if p == 0:
                dve.wait_ge(sem("z_act"), it)
            V.scalar_tensor_tensor(yb[:, p % 2, :], xs[:, p, :], gp_side[:, 4 + p:5 + p],
                                       bank(7 - p % 2)[:, 0:SEQ], ALU.mult, ALU.add).then_inc(sem("y_skip"), 1)
            dve.wait_ge(sem("y_skip"), it * 4 - 3 + p)
            V.tensor_tensor(z[:, p, :], z[:, p, :], yb[:, p % 2, :], ALU.mult).then_inc(sem("yz"), 1)

        def ssm_side(it, c_):
            if c_ == 3:
                V.tensor_copy(gp_side[:, :], gp_all[:, bass.ds(it - 1, 1), 30:38]
                                  .rearrange("p a n -> p (a n)")).then_inc(sem("gps"), 1)
                hh = bass.ds(it * HPG - HPG, HPG)
                V.tensor_copy(cum_g[:, :, :], cum_tok[:, :, hh]).then_inc(sem("gps"), 1)
                V.tensor_copy(dt_g[:, :, :], dt_tok[:, :, hh]).then_inc(sem("gps"), 1)
                dve.wait_ge(sem("cb_mm"), it)
                diag = cbm[:, :].rearrange("p (q n) -> p q n", q=3)
                V.tensor_tensor(diag[:, 0:3:2, :],
                                    bank(6)[:, 0:384].rearrange("p (q n) -> p q n", q=3)[:, 0:3:2, :],
                                    tri.unsqueeze(1).to_broadcast([P, 2, P]), ALU.mult).then_inc(sem("cbd"), 1)
                V.tensor_copy(diag[:, 1, :], bank(6)[:, 128:256]).then_inc(sem("cbm_ev"), 1)
                dve.wait_ge(sem("gps"), it * 3)
                x_dt(it, 0)
            if c_ == 4:
                dve.wait_ge(sem("cumb_in"), it * 16)
                decays(it, 0)
            if c_ == 5:
                dve.wait_ge(sem("cbm_ev"), it)
                mask_scores(it, 0)
                decays(it, 1)
            if c_ == 6:
                x_dt(it, 1)
                mask_scores(it, 1)
            if c_ == 8:
                y_gate(it, 0)
                decays(it, 2)
            if c_ == 9:
                mask_scores(it, 2)
            if c_ == 10:
                y_gate(it, 1)
                decays(it, 3)
            if c_ == 11:
                mask_scores(it, 3)
            if c_ == 12:
                y_gate(it, 2)
            if c_ == 14:
                y_gate(it, 3)
            if c_ == 17:
                dve.wait_ge(sem("ss_mm"), it)
                V.tensor_scalar(rs[:, 0, :], bank(7)[:, 0:SEQ], 1.0 / 512, EPS, ALU.mult, ALU.add) \
                    .then_inc(sem("ms"), 1)
            if c_ == 18:
                dve.wait_ge(sem("r0"), it)
                V.tensor_tensor(rs[:, 2, :], rs[:, 1, :], rs[:, 1, :], ALU.mult).then_inc(sem("nt"), 1)
                dve.wait_ge(sem("nt"), it * 3 - 2)
                V.scalar_tensor_tensor(rs[:, 2, :], rs[:, 2, :], -0.5, rs[:, 0, :], ALU.mult, ALU.mult) \
                    .then_inc(sem("nt"), 1)
                dve.wait_ge(sem("nt"), it * 3 - 1)
                V.scalar_tensor_tensor(rs[:, 2, :], rs[:, 2, :], 1.5, rs[:, 1, :], ALU.add, ALU.mult) \
                    .then_inc(sem("nt"), 1)
                dve.wait_ge(sem("nt"), it * 3)
                for t in range(4):
                    V.scalar_tensor_tensor(z[:, t, :], z[:, t, :], gp_side[:, t:t + 1], rs[:, 2, :],
                                               ALU.mult, ALU.mult).then_inc(sem("yn"), 1)
            if c_ == 19:
                dve.wait_ge(sem("ssm_hi"), it)
                tiles = bass.ds(it * 4 - 4, 4)
                V.tensor_tensor(g[:, tiles, 1, :], z[:, :, :], g[:, tiles, 0, :].bitcast(F32), ALU.subtract) \
                    .then_inc(sem("ssm_lo"), 1)

        for c_ in range(20):
            split("ssm", 0, c_)
            if c_ == 1:
                prepare_dt()
            if c_ == 4:
                softplus()
            ssm_main(0, c_)
            if c_ == 15:
                dve.wait_ge(sem("cum_mm"), 1)
                V.tensor_copy(cum_tok[:, :, :].rearrange("p b h -> p (b h)"), bank(6)[:, 0:128]) \
                    .then_inc(sem("cum_ev"), 1)
                dve.wait_ge(sem("cumt_ev"), 1)
        with dve.Fori(1, GROUPS) as it:
            for c_ in range(20):
                split("ssm", it, c_)
                ssm_side(it, c_)
                ssm_main(it, c_)

        def split_c(q):
            b = (4, 0, 2, 4)[q]
            dve.wait_ge(sem("c_sq"), q + 1)
            for i in range(2):
                t = 2 * q + i
                col = (V_QN if t < 4 else V_KVN) + t % 4
                V.scalar_tensor_tensor(c[:, t, 1, :], bank(b + i)[:, 0:SEQ], pv[:, col:col + 1],
                                           c[:, t, 0, :].bitcast(F32), ALU.mult, ALU.subtract) \
                                               .then_inc(sem("c_lo"), 1)
            acc = acc_q[:, q // 2, :]
            if q % 2 == 0:
                V.tensor_tensor(acc, sqc[:, 0, :], sqc[:, 1, :], ALU.add).then_inc(sem("accq"), 1)
            else:
                V.tensor_tensor(acc, acc, sqc[:, 0, :], ALU.add).then_inc(sem("accq"), 1)
                dve.wait_ge(sem("accq"), ACCQ[q] + 1)
                V.tensor_tensor(acc, acc, sqc[:, 1, :], ALU.add).then_inc(sem("accq"), 1)

        for c_ in range(20):
            split(*(("cq", 0, c_) if c_ < 16 else ("so", 0, c_ - 16)))
            ssm_side(GROUPS, c_)
            if c_ in (7, 11, 15, 19):
                split_c((7, 11, 15, 19).index(c_))

        def so_evac(it):
            group_end("so", it, 11)
            dve.wait_ge(sem("sg_so"), it + 1 + CREDIT["sg_so"])
            V.tensor_tensor(m[:, bass.ds(it * 2, 2), :], psum[:, 2:4, 0:SEQ], sg[:, :, :], ALU.mult) \
                .then_inc(sem("so_ev"), 1)

        TWO_PI = 2.0 * np.pi
        C1 = 6.28125
        C2 = float(np.float32(round((TWO_PI - C1) * 2.0 ** 22) / 2.0 ** 22))
        C3 = TWO_PI - C1 - C2
        ROUND = 1.5 * 2.0 ** 23

        def angle(dst, turn):
            link(V.tensor_scalar(a_k[:, :], a_ang[:, :], 1.0 / TWO_PI, turn, ALU.mult, ALU.add))
            link(V.tensor_scalar(a_k[:, :], a_k[:, :], ROUND, ROUND, ALU.add, ALU.subtract))
            link(V.scalar_tensor_tensor(dst, a_k[:, :], -C1, a_ang[:, :], ALU.mult, ALU.add))
            link(V.scalar_tensor_tensor(dst, a_k[:, :], -C2, dst, ALU.mult, ALU.add))
            link(V.scalar_tensor_tensor(dst, a_k[:, :], -C3, dst, ALU.mult, ALU.add))
            if turn:
                link(V.tensor_scalar(dst, dst, turn * TWO_PI, None, ALU.add))
            V.tensor_scalar(dst, dst, 3.1415925, -3.1415925, ALU.min, ALU.max).then_inc(sem("angles"), 1)

        for c_ in range(4, 12):
            split("so", 0, c_)
            if c_ == 4:
                for k in range(2):
                    dve.wait_ge(sem("ssqkv_mm"), k + 1)
                    V.tensor_scalar(rs[:, k, :], bank(6 + k)[:, 0:SEQ], 1.0 / Q_LORA, EPS, ALU.mult, ALU.add) \
                        .then_inc(sem("qkv_ms"), 1)
            if c_ == 5:
                for k, r in ((0, r_q), (1, r_kv)):
                    dve.wait_ge(sem("qkv_r0"), k + 1)
                    newton(rs[:, k, :], r, rs[:, 2, :], "rkv_ready" if k else None, dst=r)
                dve.wait_ge(sem("rkv_ready"), 1)
            if c_ == 6:
                dve.wait_ge(sem("pos_in"), 16)
                dve.wait_ge(sem("rope_in"), 16)
                link(V.tensor_copy(a_k[:, :], pos_i[:, :]))
                link(V.tensor_scalar(a_ang[:, :], a_k[:, :], invf, None, ALU.mult))
                angle(a_s[:, :], 0.0)
            if c_ == 7:
                dve.wait_ge(sem("angles"), 1)
                angle(a_c[:, :], 0.25)
        with dve.Fori(1, 8) as it:
            for c_ in range(12):
                split("so", it, c_)
                if c_ == 2:
                    so_evac(it - 1)

        def attn_rest(it):
            dve.wait_ge(sem("o_hi"), it - 1)
            tiles = bass.ds(it * 2 - 4, 2)
            V.tensor_tensor(g[:, tiles, 1, :], psum[:, 4:6, 0:SEQ], g[:, tiles, 0, :].bitcast(F32),
                                ALU.subtract).then_inc(sem("o_lo"), 1)

        def keys_values(it, hd):
            b = 3 if hd == 0 else 1
            group_end("at", it - 1, 2 + hd)
            if hd == 0:
                if isinstance(it, int) and it == 1:
                    pass
                else:
                    dve.wait_ge(sem("av_mm"), it * 2 - 2)
            V.tensor_tensor(kn[:, hd, :], bank(b)[:, 0:SEQ], r_kv, ALU.mult).then_inc(sem("kn_ev"), 1)
            V.tensor_tensor(vt[:, hd, :, :], bank(b)[:, SEQ:2 * SEQ].rearrange("p (b n) -> p b n", b=2),
                                rkv_tok[:, :].unsqueeze(2).to_broadcast([P, 2, VDIM]), ALU.mult) \
                                    .then_inc(sem("kv_ev"), 1)

        def rotate(it):
            dve.wait_ge(sem("rot_mm"), it)
            V.tensor_tensor(rt[:, 0, :], qp[:, :], cos[:, :], ALU.mult).then_inc(sem("rope_t"), 1)
            V.tensor_tensor(rt[:, 1, :], bank(6)[:, 0:SEQ], sin[:, :], ALU.mult).then_inc(sem("rope_t"), 1)
            dve.wait_ge(sem("rope_t"), it * 2)
            if not (isinstance(it, int) and it == 1):
                dve.wait_ge(sem("scores_mm"), it * 2 - 2)
            for hd in range(2):
                half = slice(64 * hd, 64 * hd + 64)
                V.tensor_tensor(qr[half, hd, :], rt[half, 0, :], rt[half, 1, :], ALU.add) \
                    .then_inc(sem("rope_done"), 1)

        def attn_max(it):
            for hd in range(2):
                dve.wait_ge(sem("scores_mm"), it * 2 - 1 + hd)
                V.memset(pad[:, :], 0.0)
                for q, o, n in ((0, 0, 128), (1, 128, 256)):
                    V.tensor_tensor_reduce(out=sc[:, hd, o:o + n], in0=bank(4 + hd)[:, o:o + n],
                                               in1=mask_a[:, o:o + n], scale=1.0, scalar=-3.0e38,
                                               op0=ALU.add, op1=ALU.max, accum_out=mx[:, hd, q:q + 1]) \
                                                   .then_inc(sem("rowmax"), 1)
                dve.wait_ge(sem("rowmax"), it * 4 - 2 + 2 * hd)
                V.tensor_scalar(nm[:, hd, :], mx[:, hd, :], -SCALE, None, ALU.mult).then_inc(sem("smax"), 1)

        def attn_norm(it):
            for hd in range(2):
                dve.wait_ge(sem("pexp"), it * 4 - 2 + 2 * hd)
                V.reciprocal(rl[:, hd, :], ls[:, hd, :]).then_inc(sem("rsum"), 1)
                dve.wait_ge(sem("rsum"), it * 2 - 1 + hd)
                V.tensor_scalar(sc[:, hd, 0:128], sc[:, hd, 0:128], rl[:, hd, 0:1], None, ALU.mult)
                V.tensor_scalar(sc[:, hd, 128:384], sc[:, hd, 128:384], rl[:, hd, 1:2], None, ALU.mult) \
                    .then_inc(sem("pn"), 1)

        def queries(it):
            group_end("at", it, 1)
            if not (isinstance(it, int) and it == 0):
                dve.wait_ge(sem("scores_mm"), it * 2)
            V.tensor_tensor(qp[:, :], bank(2)[:, 0:SEQ], r_q, ALU.mult).then_inc(sem("qp_ev"), 1)
            V.tensor_tensor(qn[:, :, :], bank(0)[:, :].rearrange("p (a n) -> p a n", a=2), both(r_q), ALU.mult) \
                .then_inc(sem("q_ev"), 1)

        def attn_side(it, c_):
            if c_ == 0:
                if not (isinstance(it, int) and it < 2):
                    attn_rest(it)
                keys_values(it, 0)
            if c_ == 1:
                keys_values(it, 1)
                rotate(it)
            if c_ == 2:
                attn_max(it)
            if c_ == 3:
                attn_norm(it)

        for c_ in range(4):
            split("at", 0, c_)
            if c_ == 0:
                dve.wait_ge(sem("rope_tab"), 1)
                dve.wait_ge(sem("krot_mm"), 1)
                link(V.tensor_tensor(a_s[:, :], bank(4)[:, 0:SEQ], sin[:, :], ALU.mult))
                link(V.tensor_tensor(kpe[:, :], kr, cos[:, :], ALU.mult))
                link(V.tensor_tensor(kpe[:, :], kpe[:, :], a_s[:, :], ALU.add))
                link(V.memset(qr[:, :, :], 0.0))
                dve.wait_ge(sem("rkvt_mm"), 1)
                V.tensor_copy(rkv_tok[:, :], bank(5)[:, 0:256:128]).then_inc(sem("rkvt_ev"), 1)
            if c_ == 2:
                so_evac(7)
            if c_ == 3:
                queries(0)
        for c_ in range(4):
            split("at", 1, c_)
            attn_side(1, c_)
            if c_ == 3:
                queries(1)
        with dve.Fori(2, 8) as it:
            for c_ in range(4):
                split("at", it, c_)
                attn_side(it, c_)
                if c_ == 3:
                    queries(it)

        def ao_evac(it):
            group_end("ao", it, 7)
            dve.wait_ge(sem("sg_ao"), it + 1 + CREDIT["sg_ao"])
            V.tensor_tensor(prod[:, :, :], psum[:, 2:4, 0:SEQ], sg[:, :, :], ALU.mult).then_inc(sem("ao_ev"), 1)
            dve.wait_ge(sem("ao_ev"), it + 1 + CREDIT["ao_ev"])
            V.tensor_tensor(prod[:, :, :], prod[:, :, :], m[:, bass.ds(it * 2, 2), :], ALU.add) \
                .then_inc(sem("mixed"), 1)

        def ao_rest(it):
            dve.wait_ge(sem("ao_hi"), it + 1)
            tiles = bass.ds(it * 2 + 16, 2)
            V.tensor_tensor(g[:, tiles, 1, :], prod[:, :, :], g[:, tiles, 0, :].bitcast(F32), ALU.subtract) \
                .then_inc(sem("ao_lo"), 1)

        for c_ in range(8):
            split("ao", 0, c_)
            if c_ < 4:
                attn_side(8, c_)
            if c_ == 4:
                attn_rest(9)
        with dve.Fori(1, 8) as it:
            for c_ in range(8):
                split("ao", it, c_)
                if c_ == 2:
                    ao_evac(it - 1)
                if c_ == 3:
                    ao_rest(it - 1)

        def add_squares(phase, k, sq_t, acc):
            dve.wait_ge(sem(phase + "_sq"), k + 1)
            V.tensor_tensor(acc[:, :, :], acc[:, :, :], sq_t, ALU.add).then_inc(sem(phase + "_acc"), 1)

        def wo_side(it, c_):
            if c_ == 7:
                add_squares("wo", it * 2, sq_n[:, 0, :, :], acc_n)
            if c_ == 3 and not (isinstance(it, int) and it == 0):
                add_squares("wo", it * 2 - 1, sq_n[:, 0, :, :], acc_n)

        for c_ in range(8):
            split("wo", 0, c_)
            if c_ == 1:
                dve.wait_ge(sem("chunk_done"), BASE["wo"])
                link(V.memset(acc_n[:, :, :], 0.0))
            if c_ == 2:
                ao_evac(7)
            if c_ == 3:
                ao_rest(7)
            wo_side(0, c_)
        with dve.Fori(1, 4) as it:
            for c_ in range(8):
                split("wo", it, c_)
                wo_side(it, c_)
        for c_ in range(4):
            split("ff", 0, c_)
        wo_side(4, 3)

        def total(n, b):
            dve.wait_ge(sem("tot_mm"), n)
            V.tensor_scalar(keep[:, 0, :], bank(b)[:, 0:SEQ], 1.0 / D_MODEL, EPS, ALU.mult, ALU.add) \
                .then_inc(sem("tot_ms"), 1)
            dve.wait_ge(sem("tot_r0"), n)
            newton(keep[:, 0, :], keep[:, 1, :], keep[:, 2, :], None)

        def residual(step, src, w_post, w_next, extra=None):
            for j in range(8):
                if extra:
                    extra(j)
                if j and w_next is None:
                    dve.wait_ge(sem("h_new"), 8 * step + j)
                for k in range(2):
                    kt = 2 * j + k
                    ins = V.scalar_tensor_tensor(bt[:, k, :], src[:, kt, :], pv[:, w_post + kt:w_post + kt + 1],
                                                 keep[:, 2, :], ALU.mult, ALU.mult)
                    if k:
                        link(ins)
                    else:
                        ins.then_inc(sem("bt"), 1)
                dve.wait_ge(sem("bt"), 8 * step + j + 1)
                V.tensor_tensor(h[:, 2 * j:2 * j + 2, :], h[:, 2 * j:2 * j + 2, :], bt[:, :, :], ALU.add) \
                    .then_inc(sem("h_new"), 1)
                if w_next is None:
                    continue
                dve.wait_ge(sem("u_hi"), KT * (step + 1) + 2 * j + 2)
                for k in range(2):
                    kt = 2 * j + k
                    V.scalar_tensor_tensor(u[:, kt, 1, :], h[:, kt, :], pv[:, w_next + kt:w_next + kt + 1],
                                               u[:, kt, 0, :].bitcast(F32), ALU.mult, ALU.subtract) \
                                                   .then_inc(sem("u_lo"), 1)

        def hidden_norm(n):
            dve.wait_ge(sem("hss_mm"), 8 * n)
            V.tensor_scalar(keep[:, 0, :], bank(6)[:, 0:SEQ], 1.0 / D_MODEL, EPS, ALU.mult, ALU.add) \
                .then_inc(sem("hn_ms"), 1)
            dve.wait_ge(sem("hn_r0"), n)
            newton(keep[:, 0, :], keep[:, 1, :], keep[:, 2, :], None)

        dve.wait_ge(sem("h_ev"), 8)
        total(1, 7)
        residual(0, m, V_MIXPOST, V_FFPRE)

        def ff_side(it, c_):
            if c_ == 6:
                group_end("ff", it, 3)
                V.tensor_tensor(fg[:, :, :], psum[:, 0:2, 0:SEQ], both(keep[:, 2, :]), ALU.mult) \
                    .then_inc(sem("ffg_ev"), 1)
            if isinstance(it, int) and it == 0:
                return
            if c_ == 2:
                group_end("ff", it - 1, 7)
                V.tensor_tensor(fu[:, :, :], psum[:, 2:4, 0:SEQ], both(keep[:, 2, :]), ALU.mult) \
                    .then_inc(sem("ffu_ev"), 1)
                dve.wait_ge(sem("ff_act"), it)
                dve.wait_ge(sem("ffu_ev"), it + CREDIT["ffu_ev"])
                V.tensor_tensor(fu[:, :, :], fu[:, :, :], fg[:, :, :], ALU.mult).then_inc(sem("ff_prod"), 1)
            if c_ == 3:
                dve.wait_ge(sem("ff_hi"), it)
                tiles = bass.ds(it * 2 - 2, 2)
                V.tensor_tensor(g[:, tiles, 1, :], fu[:, :, :], g[:, tiles, 0, :].bitcast(F32), ALU.subtract) \
                    .then_inc(sem("ff_lo"), 1)

        for c_ in range(4, 8):
            split("ff", 0, c_)
            if c_ == 5:
                hidden_norm(1)
            ff_side(0, c_)
        with dve.Fori(1, 22) as it:
            for c_ in range(8):
                split("ff", it, c_)
                ff_side(it, c_)

        def dn_side(it, c_):
            if c_ == 15:
                add_squares("dn", it * 2, sq_d[:, :, :], acc_d)
            if c_ == 3 and not (isinstance(it, int) and it == 0):
                add_squares("dn", it * 2 - 1, sq_d[:, :, :], acc_d)

        for c_ in range(24):
            split("dn", 0, c_)
            if c_ in (2, 3):
                ff_side(22, c_)
            if c_ == 4:
                link(V.memset(acc_d[:, :, :], 0.0))
            dn_side(0, c_)
        with dve.Fori(1, 4) as it:
            for c_ in range(24):
                split("dn", it, c_)
                dn_side(it, c_)
        for c_ in range(4):
            split("pl", 0, c_)
        dve.wait_ge(sem("pc_hi"), 1)
        V.tensor_tensor(pc[:, :, 1, :], bank(4)[:, :].rearrange("p (k s) -> p k s", k=2),
                            pc[:, :, 0, :].bitcast(F32), ALU.subtract).then_inc(sem("pc_lo"), 1)
        dn_side(4, 3)
        total(2, 0)

        def between(j):
            if j % 2 == 0:
                split("pg", 0, j // 2)
        residual(1, m, V_FFPOST, V_PLPRE, between)

        def pg_gate(k, last_chunk, b):
            group_end("pg", *last_chunk)
            V.tensor_tensor(ga[:, :, :], psum[:, b:b + 2, 0:SEQ], both(keep[:, 2, :]), ALU.mult) \
                .then_inc(sem("pg_ev"), 1)

        def pg_mul(k, tile):
            dve.wait_ge(sem("pg_act"), k + 1)
            tiles = bass.ds(tile, 2)
            V.tensor_tensor(ee[:, tiles, :], ee[:, tiles, :], ga[:, :, :], ALU.mult).then_inc(sem("pg_e"), 1)

        def pg_iter(it, c_):
            later = not (isinstance(it, int) and it == 0)
            if c_ == 6:
                pg_gate(it * 2, (it, 3), 0)
            if c_ == 7:
                pg_mul(it * 2, it * 4)
            if c_ == 0 and later:
                add_squares("pg", it * 2 - 2, sq_n[:, 0, :, :], acc_n)
            if c_ == 2 and later:
                pg_gate(it * 2 - 1, (it - 1, 7), 2)
            if c_ == 3 and later:
                pg_mul(it * 2 - 1, it * 4 - 2)
            if c_ == 4 and later:
                add_squares("pg", it * 2 - 1, sq_n[:, 0, :, :], acc_n)

        for c_ in range(4, 8):
            split("pg", 0, c_)
            if c_ == 5:
                hidden_norm(2)
                link(V.memset(acc_n[:, :, :], 0.0))
            pg_iter(0, c_)
        with dve.Fori(1, 4) as it:
            for c_ in range(8):
                split("pg", it, c_)
                pg_iter(it, c_)
        for c_ in (0, 2, 3, 4):
            pg_iter(4, c_)
        total(3, 4)
        residual(2, ee, V_PLPOST, None)

    ctx.close()


INPUTS = ["x", "p", "positions", "mix_norm_pre", "mix_norm_post", "w_in", "q_norm", "w_uq", "kv_norm", "w_ukv",
          "conv_w", "conv_b", "dt_bias", "a_log", "d_skip", "ssm_norm", "w_attn_o", "w_ssm_o", "w_out",
          "ffn_norm_pre", "ffn_norm_post", "w_gate", "w_up", "w_down",
          "ple_norm_pre", "ple_norm_post", "w_ple_gate", "w_ple"]


def kernel(**inputs):
    import concourse.bacc as bacc
    from concourse.bass_utils import run_bass_kernel_spmd

    nc = bacc.Bacc("TRN2", target_bir_lowering=False, num_devices=1)
    arrays, args = {}, []

    def give(name, a):
        arrays[name] = a
        args.append(nc.dram_tensor(name, a.shape, mybir.dt.from_np(a.dtype), kind="ExternalInput").ap())

    for name in INPUTS:
        a = np.ascontiguousarray(inputs[name])
        while a.ndim > 1 and a.shape[0] == 1:
            a = a[0]
        give(name + "_in", a)
    i = np.arange(P)
    low = (i[:, None] <= i[None, :]).astype(np.float32)
    give("constants", np.concatenate([np.eye(P, dtype=np.float32), low, np.ones((P, P), np.float32)], 1))
    later = np.where(i[None, :] > i[:, None], np.float32(NEG), np.float32(0))
    mask = np.concatenate([later, np.zeros((P, P), np.float32), later], 1)
    rot = np.zeros((P, P), np.float32)
    for half in range(2):
        for f in range(ROPE // 2):
            a, b = 64 * half + f, 64 * half + f + ROPE // 2
            rot[b, a], rot[a, b] = -1.0, 1.0
    freq = (np.float32(THETA) ** (-np.arange(0, ROPE, 2, dtype=np.float32) / np.float32(ROPE))).astype(np.float32)
    give("rotary", np.concatenate([mask, rot, np.tile(freq, 4)[:, None]], 1).astype(np.float32))
    out = nc.dram_tensor("out", (SEQ, D_MODEL), F32, kind="ExternalOutput").ap()
    build(nc, *args, out)
    got = run_bass_kernel_spmd(nc, [arrays], core_ids=[0]).results[0]["out"]
    return got.reshape(1, SEQ, D_MODEL)
```

```python
from contextlib import ExitStack

import numpy as np
import concourse.bass as bass
from concourse import mybir

F32 = mybir.dt.float32
F32R = mybir.dt.float32r
I32 = mybir.dt.int32
ALU = mybir.AluOpType
ACT = mybir.ActivationFunctionType

D_MODEL, SEQ, PLE_DIM, EPS = 2048, 256, 256, 1e-6
HEADS, Q_LORA, KV_LORA, NOPE, ROPE, VDIM = 16, 512, 512, 128, 64, 128
QK = NOPE + ROPE
SCALE = float(QK) ** -0.5
THETA = 10000.0
D_INNER, GROUPS, STATE, PDIM = 4096, 8, 128, 64
HEADS_SSM = D_INNER // PDIM
HPG = HEADS_SSM // GROUPS
CONV_DIM = D_INNER + 2 * GROUPS * STATE
D_FF = ((8 * D_MODEL // 3 + 255) // 256) * 256

C_Q = 0
C_KV = C_Q + Q_LORA
C_KR = C_KV + KV_LORA
C_Z = C_KR + ROPE
C_X = C_Z + D_INNER
C_B = C_X + D_INNER
C_DT = C_X + CONV_DIM
C_GA = C_DT + HEADS_SSM
C_GS = C_GA + D_MODEL

P = 128
KT = D_MODEL // P
NEG = -1.0e30
RING = 4
CHUNK = 1024

PHASES = {
    "kr": (4, 1),
    "ssm": (20, 8),
    "cq": (16, 1),
    "so": (12, 8),
    "at": (4, 8),
    "ao": (8, 8),
    "wo": (8, 4),
    "ff": (8, 22),
    "dn": (24, 4),
    "pl": (4, 1),
    "pg": (8, 4),
}
BASE = {}
_n = 0
for _k, (_c, _i) in PHASES.items():
    BASE[_k] = _n
    _n += _c * _i
DN_KT = [4] * 8 + [3] * 4
DN_AT = [sum(DN_KT[:i]) for i in range(12)]

V_MIXPRE, V_MIXPOST, V_FFPRE, V_FFPOST, V_PLPRE, V_PLPOST, V_QN, V_KVN = 0, 16, 32, 48, 64, 80, 96, 100
V_KEEP = 104
V_CB, V_SN, V_TAP = 104, 152, 184
V_ALL = 376
GP_N = 38


def num(phase, it, c):
    return it * PHASES[phase][0] + (BASE[phase] + c)


def build(nc, x, p_in, positions, mix_norm_pre, mix_norm_post, w_in, q_norm, w_uq, kv_norm, w_ukv,
          conv_w, conv_b, dt_bias, a_log, d_skip, ssm_norm, w_attn_o, w_ssm_o, w_out,
          ffn_norm_pre, ffn_norm_post, w_gate, w_up, w_down,
          ple_norm_pre, ple_norm_post, w_ple_gate, w_ple, cst_in, rope_in, out):
    V, S, T = nc.vector, nc.scalar, nc.tensor

    START = 16512
    CONST0 = START
    RAW0 = CONST0 + 8032
    HI0 = RAW0 + RING * CHUNK * 4
    LO0 = HI0 + RING * CHUNK * 4
    U0 = LO0 + RING * CHUNK * 4
    G0 = U0 + KT * 2048
    T0 = G0 + 44 * 2048
    H0 = T0 + 16384
    END = H0 + 16384
    assert END <= 229344

    def region(start, end):
        at = [start]

        def place(name, shape, dt=F32):
            size = int(np.prod(shape[1:])) * 4
            t = nc.alloc_sbuf_tensor_at(name, list(shape), dt, offset=at[0])
            at[0] += (size + 31) // 32 * 32
            assert at[0] <= end, (name, at[0], end)
            return t
        return place

    const = region(CONST0, RAW0)
    cst = const("cst", [P, 384])
    ident, tri, ones, tri_ones = cst[:, 0:128], cst[:, 128:256], cst[:, 256:384], cst[:, 128:384]
    pv = const("pv", [P, V_KEEP])
    gp_all = const("gp_all", [P, GROUPS, GP_N])
    gp_main = const("gp_main", [P, 30])
    gp_side = const("gp_side", [P, 8])
    dt_tok = const("dt_tok", [P, 2, HEADS_SSM])
    cum_tok = const("cum_tok", [P, 2, HEADS_SSM])
    cum_g = const("cum_g", [P, 2, HPG])
    dt_g = const("dt_g", [P, 2, HPG])
    keep = const("keep", [P, 3, SEQ])
    kr, r_q, r_kv = keep[:, 0, :], keep[:, 1, :], keep[:, 2, :]
    sqc = keep[:, 1:3, :]
    rkv_tok = const("rkv_tok", [P, 2])
    pad = const("pad", [P, 1])

    def at(name, shape, offset, dt=F32):
        return nc.alloc_sbuf_tensor_at(name, list(shape), dt, offset=offset)

    raw = at("raw", [P, RING, CHUNK], RAW0)
    whi = at("whi", [P, RING, CHUNK], HI0, F32R)
    wlo = at("wlo", [P, RING, CHUNK], LO0, F32R)
    u = at("u", [P, KT, 2, SEQ], U0, F32R)
    g = at("g", [P, 44, 2, SEQ], G0, F32R)
    m = at("m", [P, KT, SEQ], T0)
    h = at("h", [P, KT, SEQ], H0)

    first = region(G0, G0 + 32 * 2048)
    x_tok = first("x_tok", [P, 2, D_MODEL])
    xn_tok = first("xn_tok", [P, 2, D_MODEL])
    sq_tok = first("sq_tok", [P, D_MODEL])
    rows = first("rows", [P, 4, P])
    pv_all = first("pv_all", [P, V_ALL])
    st0 = first("st0", [P, 8])
    prep = region(G0 + 32 * 2048, G0 + 36 * 2048)
    dtb = prep("dtb", [P, HEADS_SSM])
    alog = prep("alog", [P, HEADS_SSM])
    dsk = prep("dsk", [P, HEADS_SSM])
    d_xb, d_e, d_r, d_s, d_s2, d_q, da = (prep(n, [P, 2, HEADS_SSM])
                                          for n in ("d_xb", "d_e", "d_r", "d_s", "d_s2", "d_q", "da"))
    cumt = prep("cumt", [HEADS_SSM, SEQ])
    ssm = region(T0, END)
    acc_q = ssm("acc_q", [P, 2, SEQ])
    rs = ssm("rs", [P, 3, SEQ])
    xs = ssm("xs", [P, 6, SEQ])
    z = ssm("z", [P, 4, SEQ])
    cumb = ssm("cumb", [P, HPG, SEQ])
    cbm = ssm("cbm", [P, 384])
    xdt = ssm("xdt", [P, 2, 4, 192])
    e = at("e", [P, 4, 384], G0 + 32 * 2048)
    sq = at("sq", [P, 4, SEQ], G0 + 32 * 2048)
    yb = at("yb", [P, 2, SEQ], G0 + 35 * 2048)
    c = at("c", [P, 8, 2, SEQ], G0 + 36 * 2048, F32R)
    late = region(H0, END)
    sg = late("sg", [P, 2, SEQ])
    prod = late("prod", [P, 2, SEQ])
    cos, sin, kpe, a_ang, a_k, a_s, a_c = (late(n, [P, SEQ])
                                           for n in ("cos", "sin", "kpe", "a_ang", "a_k", "a_s", "a_c"))
    pos_i = late("pos_i", [P, SEQ], I32)
    rope_c = late("rope_c", [P, 769])
    mask_a, rotm, invf = rope_c[:, 0:384], rope_c[:, 384:512], rope_c[:, 512:513]
    rotk, dupk = rope_c[0:64, 513:641], rope_c[0:64, 641:769]
    attn = region(G0 + 16 * 2048, G0 + 32 * 2048)
    qn = attn("qn", [P, 2, SEQ])
    qp = attn("qp", [P, SEQ])
    qr = attn("qr", [P, 2, SEQ])
    rt = attn("rt", [P, 2, SEQ])
    kn = attn("kn", [P, 2, SEQ])
    vt = attn("vt", [P, 2, 2, VDIM])
    sc = attn("sc", [P, 2, 384])
    pt = attn("pt", [P, 2, 384])
    mx, nm, ls, rl = (attn(n, [P, 2, 2]) for n in ("mx", "nm", "ls", "rl"))
    x_tok2 = at("x_tok2", [P, 2, D_MODEL], G0)
    work = region(G0 + 8 * 2048, G0 + 16 * 2048)
    sq_n = work("sq_n", [P, 2, 2, SEQ])
    acc_n = work("acc_n", [P, 2, SEQ])
    bt = work("bt", [P, 2, 2, SEQ])
    fg = at("fg", [P, 2, SEQ], T0)
    fu = at("fu", [P, 2, SEQ], T0 + 2048)
    gx = at("gx", [P, 2, SEQ], T0 + 4096)
    ux = at("ux", [P, 2, SEQ], T0 + 6144)
    sq_d = at("sq_d", [P, 2, SEQ], U0)
    acc_d = at("acc_d", [P, 2, SEQ], U0 + 2048)
    dx = at("dx", [P, 2, SEQ], U0 + 4096)
    p_tok = at("p_tok", [P, 2, PLE_DIM], U0 + 12 * 2048)
    pc = at("pc", [P, 2, 2, SEQ], U0 + 14 * 2048, F32R)
    ee = at("ee", [P, KT, SEQ], G0)
    ga = at("ga", [P, 2, SEQ], G0 + 16 * 2048)
    ot = at("ot", [P, 2, D_MODEL], G0 + 20 * 2048)

    psum = nc.alloc_psum_tensor("acc", [P, 8, 512], F32)

    def bank(b):
        return psum[:, b, :]

    cum_dram = nc.dram_tensor("cum_scratch", [HEADS_SSM, SEQ], F32, kind="Internal").ap()

    CREDIT = {"sg_so": 1, "so_ev": 1, "sg_ao": 1, "ao_ev": 1, "wo_cp": 2, "ffg_ev": 1, "ffu_ev": 1,
              "dn_cp": 2, "pg_ev": 2, "wo_acc": 1, "dn_acc": 1, "pg_acc": 1, "ssm_lo": 1}
    ACCQ = (0, 1, 3, 4, 6)
    names = {}

    def sem(name):
        if name not in names:
            names[name] = nc.alloc_semaphore(name)
        return names[name]

    raw_in = [sem(f"raw_in{i}") for i in range(RING)]

    w_in4 = w_in.rearrange("(q t p) n -> q p t n", t=4, p=P)
    w_uq2 = w_uq.rearrange("(q t p) n -> q p t n", t=2, p=P)
    w_ukv4 = w_ukv.rearrange("(t p) n -> p t n", p=P)
    w_so4 = w_ssm_o.rearrange("(q t p) n -> q p t n", t=4, p=P)
    w_ao4 = w_attn_o.rearrange("(q t p) n -> q p t n", t=4, p=P)
    w_wo4 = w_out.rearrange("(q t p) n -> q p t n", t=4, p=P)
    w_g4 = w_gate.rearrange("(q t p) n -> q p t n", t=4, p=P)
    w_u4 = w_up.rearrange("(q t p) n -> q p t n", t=4, p=P)
    w_dn = w_down.rearrange("(t p) n -> p t n", p=P)
    w_pg4 = w_ple_gate.rearrange("(q t p) n -> q p t n", t=4, p=P)
    w_pl2 = w_ple.rearrange("(t p) n -> p t n", p=P)
    D_IN = w_in.shape[1]

    TURNS = ("ff", "pg")

    def source(phase, it, c):
        ds = bass.ds
        if phase in TURNS and isinstance(it, int):
            c = c % 2 * 4 + c // 2
        if phase == "kr":
            return [w_in4[c][:, :, first:first + 64] for first in (C_KR, C_DT)]
        if phase == "ssm":
            q, k = divmod(c, 4)
            if q == 0:
                return [w_in4[k][:, :, ds(it * STATE + first, STATE)] for first in (C_B, C_B + GROUPS * STATE)]
            first_col = {1: C_X, 2: C_X + 256, 3: C_Z, 4: C_Z + 256}[q]
            return [w_in4[k][:, :, ds(it * 512 + first_col, 256)]]
        if phase == "cq":
            q, k = divmod(c, 4)
            return [w_in4[k][:, :, 256 * q:256 * q + 256]]
        if phase == "so":
            if c < 4:
                return [w_in4[c][:, :, ds(it * 256 + C_GS, 256)]]
            return [w_so4[c - 4][:, :, ds(it * 256, 256)]]
        if phase == "at":
            if c < 2:
                return [w_uq2[c][:, :, ds(it * (2 * QK) + first, n)]
                        for first, n in ((0, NOPE), (QK, NOPE), (NOPE, ROPE), (QK + NOPE, ROPE))]
            return [w_ukv4[:, :, ds(it * 512 + 256 * hd + NOPE * (c - 2), NOPE)] for hd in range(2)]
        if phase == "ao":
            if c < 4:
                return [w_in4[c][:, :, ds(it * 256 + C_GA, 256)]]
            return [w_ao4[c - 4][:, :, ds(it * 256, 256)]]
        if phase == "wo":
            q, k = divmod(c, 4)
            return [w_wo4[k][:, :, ds(it * 512 + 256 * q, 256)]]
        if phase == "ff":
            return [(w_g4 if c < 4 else w_u4)[c % 4][:, :, ds(it * 256, 256)]]
        if phase == "dn":
            q, k = divmod(c, 12)
            return [w_dn[:, DN_AT[k]:DN_AT[k] + DN_KT[k], ds(it * 512 + 256 * q, 256)]]
        if phase == "pl":
            return [w_pl2[:, :, 512 * c:512 * c + 512]]
        q, k = divmod(c, 4)
        return [w_pg4[k][:, :, ds(it * 512 + 256 * q, 256)]]

    FIRST_COLUMN = {"so": (4,), "at": (0, 2), "ao": (4,), "wo": (0,), "ff": (0, 4), "dn": (0,), "pg": (0,)}

    def width(phase, c):
        if phase == "kr":
            return 4 * P
        if phase == "at" and c < 2:
            return 2 * 2 * QK
        if phase == "dn":
            return DN_KT[c % 12] * 256
        return CHUNK

    def loads(phase, it, c):
        n = it * (PHASES[phase][0] // RING) + (BASE[phase] // RING + c // RING + 2)
        if phase == "kr":
            return n
        if phase == "ssm":
            return n + (it + 1)
        n = n + GROUPS
        if phase == "cq" or phase == "so":
            return n
        more = 3 if c % RING < 2 else 1
        return n + more * (it + 1) if phase == "at" else n + more * PHASES["at"][1]

    ctx = ExitStack()
    block = ctx.enter_context(nc.Block())

    @block.sync
    def _(sp):
        x_view = x.rearrange("(b p) d -> b p d", p=P)
        for b in range(2):
            sp.dma_start(x_tok[:, b, :], x_view[b]).then_inc(sem(f"x_in{b}"), 16)
        sp.dma_start(cst[:, :], cst_in).then_inc(sem("cst_in"), 16)
        vec = [(mix_norm_pre, 16, 0), (mix_norm_post, 16, 16), (ffn_norm_pre, 16, 32), (ffn_norm_post, 16, 48),
               (ple_norm_pre, 16, 64), (ple_norm_post, 16, 80), (q_norm, 4, 96), (kv_norm, 4, 100)]
        for v, n, at_row in vec:
            sp.dma_start(rows[at_row:at_row + n, 0, :], v.rearrange("(t p) -> t p", p=P)) \
                .then_inc(sem("rows_in"), 16)
        sp.dma_start(rows[0:48, 1, :], conv_b.rearrange("(t p) -> t p", p=P)).then_inc(sem("rows_in"), 16)
        sp.dma_start(rows[48:80, 1, :], ssm_norm.rearrange("(t p) -> t p", p=P)).then_inc(sem("rows_in"), 16)
        for i in range(2):
            sp.dma_start(rows[0:96, 2 + i, :],
                         conv_w[2 * i:2 * i + 2, :].rearrange("a (t p) -> (a t) p", p=P)) \
                .then_inc(sem("rows_in"), 16)
        for phase, (per, its) in PHASES.items():
            def load(it, c):
                slot = c % RING
                w = width(phase, c)
                parts = source(phase, it, c)
                dst = raw[:, slot, 0:w].rearrange("p (t n) -> p t n", t=parts[0].shape[1])
                if phase != "kr":
                    sp.wait_ge(sem("lo_ready"), num(phase, it, c) - RING + 1)
                    if c in FIRST_COLUMN.get(phase, ()):
                        sp.sem_inc(sem("slot_free"), 1)
                o = 0
                for src in parts:
                    sp.dma_start(dst[:, :, o:o + src.shape[2]], src).then_inc(raw_in[slot], 16)
                    o += src.shape[2]
            first = 0
            if its == 1 or phase in TURNS:
                for c_ in range(per):
                    load(0, c_)
                first = 1
            if its > 1:
                with sp.Fori(first, its) as it:
                    for c_ in range(per):
                        load(it, c_)
        out_view = out.rearrange("(b p) d -> p b d", p=P)
        for q in range(4):
            sp.wait_ge(sem("ot_ready"), 2 * q + 2)
            sp.dma_start(out_view[:, :, 512 * q:512 * q + 512],
                         ot[:, :, 512 * q:512 * q + 512]).then_inc(sem("out_done"), 16)
        sp.wait_ge(sem("out_done"), 64)

    @block.gpsimd
    def _(pool):
        for v, dst in ((dt_bias, dtb), (a_log, alog), (d_skip, dsk)):
            pool.dma_start(dst[:, :], v.partition_broadcast(P)).then_inc(sem("heads_in"), 16)
        pool.wait_ge(sem("cumt_ev"), 1)
        pool.dma_start(cum_dram, cumt[:, :]).then_inc(sem("cum_out"), 16)
        pool.wait_ge(sem("cum_out"), 16)

        def load_cum(gi):
            pool.dma_start(cumb[:, :, :].rearrange("p h s -> p (h s)"),
                           cum_dram[bass.ds(gi * HPG, HPG), :].rearrange("h s -> (h s)").partition_broadcast(P)) \
                .then_inc(sem("cumb_in"), 16)
        load_cum(0)
        with pool.Fori(1, GROUPS) as gi:
            pool.wait_ge(sem("seg"), gi * (2 * HPG))
            load_cum(gi)
        pool.wait_ge(sem("ssm_lo"), GROUPS + CREDIT["ssm_lo"])
        pool.dma_start(pos_i[:, :], positions.partition_broadcast(P)).then_inc(sem("pos_in"), 16)
        pool.dma_start(rope_c[:, :], rope_in).then_inc(sem("rope_in"), 16)
        pool.wait_ge(sem("chunk_done"), BASE["wo"])
        for b in range(2):
            pool.dma_start(x_tok2[:, b, :], x.rearrange("(b p) d -> b p d", p=P)[b]) \
                .then_inc(sem("x_in2"), 16)
        pool.wait_ge(sem("chunk_done"), BASE["dn"])
        pool.dma_start(p_tok[:, :, :], p_in.rearrange("(b p) d -> p b d", p=P)).then_inc(sem("p_in"), 16)

    @block.tensor
    def _(pe):
        for name, n in CREDIT.items():
            pe.sem_inc(sem(name), n)

        def mm3(o, wh, wl, xh, xl, start, stop):
            T.matmul(o, wh, xh, start=start, stop=False, skip_group_check=True)
            T.matmul(o, wh, xl, start=False, stop=False, skip_group_check=True)
            return T.matmul(o, wl, xh, start=False, stop=stop, skip_group_check=True)

        def begin(phase, it, c):
            pe.wait_ge(sem("lo_ready"), num(phase, it, c) + 1)

        def ring(c, n):
            slot = c % RING
            return (whi[:, slot, :].rearrange("p (t n) -> p t n", n=n),
                    wlo[:, slot, :].rearrange("p (t n) -> p t n", n=n))

        def chunk(phase, it, c, banks, src, kts, start, stop, cols=256):
            begin(phase, it, c)
            wh, wl = ring(c, cols)
            for i, b in enumerate(banks):
                for j, kt in enumerate(kts):
                    if phase in ("ff", "dn"):
                        T.matmul(bank(b), wh[:, j, i * P:i * P + P], src[:, kt, :, :].rearrange("p a s -> p (a s)"),
                                 start=start and j == 0, stop=False, skip_group_check=True)
                        last = T.matmul(bank(b)[:, 0:SEQ], wl[:, j, i * P:i * P + P], src[:, kt, 0, :],
                                        start=False, stop=stop and j == len(kts) - 1, skip_group_check=True)
                        continue
                    last = mm3(bank(b)[:, 0:SEQ], wh[:, j, i * P:i * P + P], wl[:, j, i * P:i * P + P],
                               src[:, kt, 0, :], src[:, kt, 1, :],
                               start and j == 0, stop and j == len(kts) - 1)
            last.then_inc(sem("chunk_done"), 1)

        def group(phase, it, c0, banks, src, k0=0, n=4, after=None):
            for i in range(n):
                chunk(phase, it, c0 + i, banks, src, range(k0 + 4 * i, k0 + 4 * i + 4), i == 0, i == n - 1)
                if after:
                    after(i)

        pe.wait_ge(sem("cst_in"), 16)
        pe.wait_ge(sem("rows_in"), 12 * 16)
        at_col = 0
        for i, n in enumerate((V_KEEP, 80, 96, 96)):
            last = T.transpose(bank(7)[:, at_col:at_col + n], rows[0:n, i, :], cst[0:n, 0:n])
            at_col += n
        last.then_inc(sem("pv_mm"), 1)
        for b in range(8):
            if b == 0:
                pe.wait_ge(sem("xn_ready"), 2)
            if b == 7:
                pe.wait_ge(sem("pv_ev"), 1)
            for k in range(2):
                for blk in range(2):
                    kt = 2 * b + k
                    last = T.transpose(bank(b)[:, k * SEQ + blk * P:k * SEQ + blk * P + P],
                                       xn_tok[:, blk, kt * P:kt * P + P], ident)
            last.then_inc(sem("xt_mm"), 1)

        for c_ in range(4):
            begin("kr", 0, c_)
            pe.wait_ge(sem("u_lo"), max(6, 4 * c_ + 4))
            wh, wl = ring(c_, 128)
            for j in range(4):
                kt = 4 * c_ + j
                last = mm3(bank(0)[:, 0:SEQ], wh[:, j, :], wl[:, j, :], u[:, kt, 0, :], u[:, kt, 1, :],
                           kt == 0, kt == KT - 1)
            last.then_inc(sem("chunk_done"), 1)

        def dt_by_tokens():
            pe.wait_ge(sem("kr_ev"), 1)
            for blk in range(2):
                last = T.transpose(bank(1 + blk)[:, 0:64], kr[64:P, blk * P:blk * P + P], cst[64:P, 64:P])
            last.then_inc(sem("dt_mm"), 1)

        def cum_sums():
            pe.wait_ge(sem("da_ready"), 1)
            T.matmul(bank(6)[:, 0:64], tri, da[:, 0, :], start=True, stop=True)
            T.matmul(bank(6)[:, 64:128], ones, da[:, 0, :], start=True, stop=False)
            T.matmul(bank(6)[:, 64:128], tri, da[:, 1, :], start=False, stop=True).then_inc(sem("cum_mm"), 1)
            T.matmul(bank(7)[0:64, 0:SEQ], da[:, 0, :], tri_ones, start=True, stop=False)
            T.matmul(bank(7)[0:64, P:SEQ], da[:, 1, :], tri, start=False, stop=True).then_inc(sem("cum_mm"), 1)

        def ssd_step(it, c_):
            if c_ == 0:
                pe.wait_ge(sem("xs_act"), it)
                T.matmul(bank(6)[:, 0:256], xs[:, 4, 0:128], xs[:, 5, :], start=True, stop=True)
                T.matmul(bank(6)[:, 256:384], xs[:, 4, 128:256], xs[:, 5, 128:256], start=True, stop=True) \
                    .then_inc(sem("cb_mm"), 1)
            if c_ in (0, 3):
                blk = c_ // 3
                if blk:
                    pe.wait_ge(sem("cbm_ev"), it)
                for t in range(4):
                    last = T.transpose(bank(7 - blk)[:, t * P:t * P + P], xs[:, t, blk * P:blk * P + P], ident)
                last.then_inc(sem("xtr_mm"), 1)
            if c_ in (5, 7, 9, 11):
                p = (c_ - 5) // 2
                b = 7 - p % 2
                if p == 0:
                    pe.wait_ge(sem("xdt_ready"), it * 2)
                if p >= 2:
                    pe.wait_ge(sem("y_skip"), it * 4 - 4 + p - 1)
                pe.wait_ge(sem("masked"), it * 8 - 8 + 2 * p + 2)
                ea, eb = e[:, 2 * p % 4, :], e[:, (2 * p + 1) % 4, :]
                T.matmul(bank(b)[:, 0:256], xdt[:, 0, p, 0:128], ea[:, 0:256], start=True, stop=False,
                         skip_group_check=True)
                T.matmul(bank(b)[:, 128:256], xdt[:, 1, p, 0:128], ea[:, 256:384], start=False, stop=False,
                         skip_group_check=True)
                T.matmul(bank(b)[:, 128:256], xdt[:, 1, p, 64:192], eb[:, 256:384], start=False, stop=False,
                         skip_group_check=True)
                T.matmul(bank(b)[:, 0:256], xdt[:, 0, p, 64:192], eb[:, 0:256], start=False, stop=True,
                             skip_group_check=True).then_inc(sem("y_mm"), 1)
            if c_ == 14:
                pe.wait_ge(sem("sq_ready"), it)
                for t in range(4):
                    last = T.matmul(bank(7)[:, 0:256], ones, sq[:, t, :], start=t == 0, stop=t == 3)
                last.then_inc(sem("ss_mm"), 1)

        def ssm_group(it):
            head = isinstance(it, int)
            for c_ in range(20):
                q, k = divmod(c_, 4)
                banks = ((4, 5), (0, 1), (2, 3), (0, 1), (2, 3))[q]
                if k == 0:
                    if q == 0 and not head:
                        pe.wait_ge(sem("conv_done"), it * 6 - 4)
                    if q == 1 and head:
                        pe.wait_ge(sem("kr_ev"), 1)
                        pe.wait_ge(sem("dt_xb"), 2)
                    if q in (1, 2) and not head:
                        pe.wait_ge(sem("z_act"), it)
                    if q == 3:
                        pe.wait_ge(sem("conv_done"), it * 6 + 4)
                    if q == 4:
                        pe.wait_ge(sem("conv_done"), it * 6 + 6)
                chunk("ssm", it, c_, banks, u, range(4 * k, 4 * k + 4), k == 0, k == 3)
                if head and c_ == 0:
                    dt_by_tokens()
                if head and c_ == 11:
                    cum_sums()
                if not head:
                    ssd_step(it, c_)

        ssm_group(0)
        with pe.Fori(1, GROUPS) as it:
            ssm_group(it)

        for c_ in range(16):
            q, k = divmod(c_, 4)
            banks = ((4, 5), (0, 1), (2, 3), (4, 5))[q]
            if k == 0 and q == 0:
                pe.wait_ge(sem("conv_done"), GROUPS * 6 - 4)
            if k == 0 and q in (1, 2):
                pe.wait_ge(sem("z_act"), GROUPS)
            if k == 0 and q == 3:
                pe.wait_ge(sem("c_lo"), 2)
            chunk("cq", 0, c_, banks, u, range(4 * k, 4 * k + 4), k == 0, k == 3)
            ssd_step(GROUPS, c_)

        def so_iter(it, after=None):
            pe.wait_ge(sem("sg_so"), it + CREDIT["sg_so"])
            group("so", it, 0, (0, 1), u, after=after)
            pe.wait_ge(sem("so_ev"), it + CREDIT["so_ev"])
            if isinstance(it, int):
                pe.wait_ge(sem("ssm_lo"), GROUPS + CREDIT["ssm_lo"])
            group("so", it, 4, (2, 3), g, n=8)

        def norms_qkv(i):
            if i == 3:
                pe.wait_ge(sem("accq"), ACCQ[4])
                for k in range(2):
                    pe.wait_ge(sem("ms"), GROUPS)
                    T.matmul(bank(6 + k)[:, 0:SEQ], ones, acc_q[:, k, :], start=True, stop=True) \
                        .then_inc(sem("ssqkv_mm"), 1)

        pe.wait_ge(sem("c_lo"), 6)
        so_iter(0, norms_qkv)
        pe.wait_ge(sem("rope_tab"), 1)
        pe.wait_ge(sem("c_lo"), 8)
        T.matmul(bank(4)[:, 0:SEQ], rotk, kr[0:64, :], start=True, stop=True)
        T.matmul(bank(4)[:, SEQ:2 * SEQ], dupk, kr[0:64, :], start=True, stop=True).then_inc(sem("krot_mm"), 1)
        pe.wait_ge(sem("rkv_ready"), 1)
        for blk in range(2):
            last = T.transpose(bank(5)[:, blk * P:blk * P + P], r_kv[:, blk * P:blk * P + P], ident)
        last.then_inc(sem("rkvt_mm"), 1)
        with pe.Fori(1, 8) as it:
            so_iter(it)

        def attn_rot(it):
            pe.wait_ge(sem("qp_ev"), it)
            if isinstance(it, int) and it == 1:
                pass
            else:
                pe.wait_ge(sem("pt_ev"), it * 2 - 2)
            T.matmul(bank(6)[:, 0:SEQ], rotm, qp[:, :], start=True, stop=True).then_inc(sem("rot_mm"), 1)

        def attn_scores(it):
            pe.wait_ge(sem("kn_ev"), it)
            pe.wait_ge(sem("rope_done"), it * 2)
            if isinstance(it, int) and it == 1:
                pass
            else:
                pe.wait_ge(sem("smax"), it * 2 - 2)
            for hd in range(2):
                for q, o, n in ((0, 0, 128), (1, 128, 256)):
                    t = slice(q * P, q * P + P)
                    T.matmul(bank(4 + hd)[:, o:o + n], qn[:, hd, t], kn[:, hd, 0:n], start=True, stop=False)
                    last = T.matmul(bank(4 + hd)[:, o:o + n], qr[:, hd, t], kpe[:, 0:n], start=False, stop=True)
                last.then_inc(sem("scores_mm"), 1)

        def attn_turn(it):
            for hd in range(2):
                pe.wait_ge(sem("pn"), it * 2 - 1 + hd)
                if hd == 1:
                    if isinstance(it, int) and it == 1:
                        pass
                    else:
                        pe.wait_ge(sem("o_lo"), it - 1)
                for j in range(3):
                    last = T.transpose(bank(6 + hd)[:, j * P:j * P + P], sc[:, hd, j * P:j * P + P], ident)
                last.then_inc(sem("pt_mm"), 1)

        def attn_values(it):
            pe.wait_ge(sem("pt_ev"), it * 2)
            pe.wait_ge(sem("v_ev"), it)
            for hd in range(2):
                T.matmul(bank(7)[:, hd * SEQ:hd * SEQ + SEQ], vt[:, 0, hd, :], pt[:, hd, 0:256], start=hd == 0,
                         stop=False, skip_group_check=True)
                last = T.matmul(bank(7)[:, hd * SEQ + P:hd * SEQ + SEQ], vt[:, 1, hd, :], pt[:, hd, 256:384],
                                start=False, stop=hd == 1, skip_group_check=True)
            last.then_inc(sem("av_mm"), 1)

        def attn_main(it, c_):
            begin("at", it, c_)
            if c_ < 2:
                if c_ == 0:
                    if isinstance(it, int) and it == 0:
                        pe.wait_ge(sem("sg_so"), 8 + CREDIT["sg_so"])
                        pe.wait_ge(sem("so_ev"), 8 + CREDIT["so_ev"])
                        pe.wait_ge(sem("rkvt_ev"), 1)
                    else:
                        pe.wait_ge(sem("q_ev"), it)
                wh, wl = ((w[:, c_ % RING, 0:768].rearrange("p (t n) -> p t n", n=2 * QK)) for w in (whi, wlo))
                for j in range(2):
                    kt = 2 * c_ + j
                    st, sp_ = kt == 0, kt == 3
                    x2 = (c[:, kt, 0, :], c[:, kt, 1, :])
                    for hd in range(2):
                        o = slice(hd * NOPE, hd * NOPE + NOPE)
                        mm3(bank(0)[:, hd * SEQ:hd * SEQ + SEQ], wh[:, j, o], wl[:, j, o], *x2,
                            st and hd == 0, sp_ and hd == 1)
                    o = slice(2 * NOPE, 2 * QK)
                    last = mm3(bank(2)[:, 0:SEQ], wh[:, j, o], wl[:, j, o], *x2, st, sp_)
            elif c_ == 2:
                if not (isinstance(it, int) and it == 0):
                    pe.wait_ge(sem("kn_ev"), it)
                wh, wl = ring(c_, 256)
                for j in range(4):
                    for hd in range(2):
                        o = slice(hd * NOPE, hd * NOPE + NOPE)
                        last = mm3(bank(3)[:, hd * SEQ:hd * SEQ + SEQ], wh[:, j, o], wl[:, j, o],
                                   c[:, 4 + j, 0, :], c[:, 4 + j, 1, :], j == 0 and hd == 0, j == 3 and hd == 1)
            else:
                if not (isinstance(it, int) and it == 0):
                    pe.wait_ge(sem("v_ev"), it)
                wh, wl = ring(c_, 256)
                for j in range(4):
                    for blk in range(2):
                        o, t = bank(1)[:, blk * SEQ:blk * SEQ + SEQ], slice(blk * P, blk * P + P)
                        for n_, (a_, w_) in enumerate(((0, wh), (0, wl), (1, wh))):
                            last = T.matmul(o, c[:, 4 + j, a_, t], w_[:, j, :],
                                            start=j == 0 and blk == 0 and n_ == 0,
                                            stop=j == 3 and n_ == 2 and blk == 1, skip_group_check=True)
            last.then_inc(sem("chunk_done"), 1)

        def attn_iter(it):
            attn_main(it, 0)
            if not (isinstance(it, int) and it == 1):
                attn_values(it - 1)
            attn_rot(it)
            attn_main(it, 1)
            attn_scores(it)
            attn_main(it, 2)
            attn_main(it, 3)
            attn_turn(it)

        for c_ in range(4):
            attn_main(0, c_)
        attn_iter(1)
        with pe.Fori(2, 8) as it:
            attn_iter(it)

        def ao_iter(it, after=None):
            if isinstance(it, int):
                pe.wait_ge(sem("q_ev"), 8)
                attn_values(7)
                attn_rot(8)
                pe.wait_ge(sem("v_ev"), 8)
            pe.wait_ge(sem("sg_ao"), it + CREDIT["sg_ao"])
            group("ao", it, 0, (0, 1), u, after=after)
            pe.wait_ge(sem("ao_ev"), it + CREDIT["ao_ev"])

            for i in range(4):
                if isinstance(it, int) and i == 0:
                    pe.wait_ge(sem("o_lo"), 7)
                if isinstance(it, int) and i == 3:
                    pe.wait_ge(sem("o_lo"), 8)
                chunk("ao", it, 4 + i, (2, 3), g, range(4 * i, 4 * i + 4), i == 0, i == 3)
                if isinstance(it, int) and i == 0:
                    attn_values(8)

        def last_pair(i):
            if i == 1:
                attn_scores(8)
            if i == 3:
                attn_turn(8)
        ao_iter(0, last_pair)
        with pe.Fori(1, 8) as it:
            ao_iter(it)

        def two_groups(phase, it, src, k0, free, after=None, gate=None):
            for c_ in range(8):
                q, k = divmod(c_, 4)
                if k == 0 and not (phase == "pg" and isinstance(it, int) and q == 0):
                    pe.wait_ge(sem(free), it * 2 + (q - 1) + CREDIT[free])
                if gate:
                    gate(k)
                chunk(phase, it, c_, ((0, 1), (2, 3))[q], src, range(k0 + 4 * k, k0 + 4 * k + 4), k == 0, k == 3)
                if after:
                    after(c_)

        def in_turns(phase, step):
            for c_ in range(8):
                k, q = divmod(c_, 2)
                if q == 0:
                    for j in (2 * k, 2 * k + 1):
                        pe.wait_ge(sem("hsq"), 8 * step + j + 1)
                        for i in range(2):
                            last = T.matmul(bank(6)[:, 0:SEQ], ones, sq_n[:, j % 2, i, :],
                                            start=j == 0 and i == 0, stop=j == 7 and i == 1,
                                            skip_group_check=True)
                        last.then_inc(sem("hss_mm"), 1)
                    pe.wait_ge(sem("u_lo"), KT * (step + 1) + 4 * k + 4)
                chunk(phase, 0, c_, ((4, 5), (2, 3))[q], u, range(4 * k, 4 * k + 4), k == 0, k == 3)

        def mixed_ready(k):
            pe.wait_ge(sem("ao_lo"), 2 * k + 2)

        def x_again(c_):
            if c_ in (0, 1, 4, 5):
                i = (0, 1, 4, 5).index(c_)
                if i == 0:
                    pe.wait_ge(sem("x_in2"), 32)
                    pe.wait_ge(sem("o_lo"), 8)
                for b in (4 + 2 * (i % 2), 5 + 2 * (i % 2)):
                    kt = 4 * i + 2 * (b % 2)
                    if i >= 2:
                        pe.wait_ge(sem("h_ev"), 2 * (i - 2) + b % 2 + 1)
                    for k in range(2):
                        for blk in range(2):
                            last = T.transpose(bank(b)[:, k * SEQ + blk * P:k * SEQ + blk * P + P],
                                               x_tok2[:, blk, (kt + k) * P:(kt + k) * P + P], ident)
                    last.then_inc(sem("ht_mm"), 1)

        with pe.Fori(0, 3) as it:
            two_groups("wo", it, g, 16, "wo_cp", gate=mixed_ready)
        two_groups("wo", 3, g, 16, "wo_cp", after=x_again)

        def ss_total(phase, acc, sq_t, b):
            pe.wait_ge(sem(phase + "_acc"), 7 + CREDIT[phase + "_acc"])
            for k in range(2):
                T.matmul(bank(b)[:, 0:SEQ], ones, acc[:, k, :], start=k == 0, stop=False, skip_group_check=True)
            pe.wait_ge(sem(phase + "_sq"), 8)
            for k in range(2):
                last = T.matmul(bank(b)[:, 0:SEQ], ones, sq_t[:, k, :], start=False, stop=k == 1,
                                skip_group_check=True)
            last.then_inc(sem("tot_mm"), 1)

        pe.wait_ge(sem("h_ev"), 8)
        ss_total("wo", acc_n, sq_n[:, 0, :, :], 7)
        pe.wait_ge(sem("wo_cp"), 8 + CREDIT["wo_cp"])

        def ff_iter(it):
            if not isinstance(it, int):
                pe.wait_ge(sem("ffg_ev"), it + CREDIT["ffg_ev"])
            group("ff", it, 0, (0, 1), u)
            pe.wait_ge(sem("ffu_ev"), it + CREDIT["ffu_ev"])
            group("ff", it, 4, (2, 3), u)
        in_turns("ff", 0)
        ff_iter(1)
        with pe.Fori(2, 22) as it:
            ff_iter(it)

        def dn_iter(it):
            for c_ in range(24):
                q, k = divmod(c_, 12)
                if k == 0:
                    pe.wait_ge(sem("dn_cp"), it * 2 + (q - 1) + CREDIT["dn_cp"])
                    pe.wait_ge(sem("ffu_ev"), 22 + CREDIT["ffu_ev"])
                    pe.wait_ge(sem("ff_lo"), 20)
                if isinstance(it, int) and c_ == 12:
                    pe.wait_ge(sem("p_in"), 16)
                    for i in range(2):
                        for blk in range(2):
                            last = T.transpose(bank(4)[:, i * SEQ + blk * P:i * SEQ + blk * P + P],
                                               p_tok[:, blk, i * P:i * P + P], ident)
                    last.then_inc(sem("pt8_mm"), 1)
                if k == 10:
                    pe.wait_ge(sem("ff_lo"), 21)
                if k == 11:
                    pe.wait_ge(sem("ff_lo"), 22)
                chunk("dn", it, c_, ((0, 1), (2, 3))[q], g, range(DN_AT[k], DN_AT[k] + DN_KT[k]), k == 0, k == 11)

        dn_iter(0)
        with pe.Fori(1, 4) as it:
            dn_iter(it)

        pe.wait_ge(sem("pc_lo"), 1)
        for c_ in range(4):
            if c_:
                pe.wait_ge(sem("ee_ev"), c_)
            chunk("pl", 0, c_, (4, 5, 6, 7), pc, range(2), True, True, cols=512)
            if c_ == 0:
                pe.wait_ge(sem("dn_cp"), 7 + CREDIT["dn_cp"])
                ss_total("dn", acc_d, sq_d, 0)
        pe.wait_ge(sem("ee_ev"), 4)
        pe.wait_ge(sem("dn_cp"), 8 + CREDIT["dn_cp"])
        pe.wait_ge(sem("tot_ms"), 2)

        in_turns("pg", 1)
        two_groups("pg", 1, u, 0, "pg_ev")
        with pe.Fori(2, 4) as it:
            two_groups("pg", it, u, 0, "pg_ev")
        ss_total("pg", acc_n, sq_n[:, 0, :, :], 4)
        for j in range(8):
            pe.wait_ge(sem("h_new"), 16 + j + 1)
            if j == 0:
                pe.wait_ge(sem("tot_ms"), 3)
            for blk in range(2):
                for k in range(2):
                    last = T.transpose(bank(j)[:, blk * SEQ + k * P:blk * SEQ + k * P + P],
                                       h[:, 2 * j + k, blk * P:blk * P + P], ident)
            last.then_inc(sem("ot_mm"), 1)

    @block.scalar
    def _(act):
        def split(phase, it, c):
            slot, w = c % RING, width(phase, c)
            act.wait_ge(raw_in[slot], loads(phase, it, c) * 16)
            if phase != "kr":
                act.wait_ge(sem("chunk_done"), num(phase, it, c) - RING + 1)
            S.activation(whi[:, slot, 0:w], raw[:, slot, 0:w], ACT.Copy).then_inc(sem("hi_ready"), 1)

        def group_end(phase, it, c_last):
            act.wait_ge(sem("chunk_done"), num(phase, it, c_last) + 1)

        def rstd(src, tmp, name, n):
            act.wait_ge(sem(name + "_ms"), n)
            S.activation(tmp, src, ACT.Ln).then_inc(sem(name + "_ln"), 1)
            act.wait_ge(sem(name + "_ln"), n)
            S.activation(tmp, tmp, ACT.Exp, scale=-0.5).then_inc(sem(name + "_r0"), 1)

        for b in range(2):
            act.wait_ge(sem(f"x_in{b}"), 16)
            S.activation(sq_tok[:, :], x_tok[:, b, :], ACT.Square, accum_out=st0[:, b:b + 1]) \
                .then_inc(sem("x_ssq"), 1)
            if b == 0:
                act.wait_ge(sem("x_ssq"), 1)
        rstd(st0[:, 2:4], st0[:, 4:6], "x", 1)
        act.wait_ge(sem("pv_ev"), 1)
        for b in range(8):
            act.wait_ge(sem("xt_mm"), b + 1)
            for k in range(2):
                kt = 2 * b + k
                S.activation(u[:, kt, 0, :], bank(b)[:, k * SEQ:k * SEQ + SEQ], ACT.Identity,
                                 scale=pv_all[:, V_MIXPRE + kt:V_MIXPRE + kt + 1]).then_inc(sem("u_hi"), 1)
            if b in (1, 3, 5, 6):
                split("kr", 0, (1, 3, 5, 6).index(b))
        group_end("kr", 0, 3)
        S.activation(kr, bank(0)[:, 0:SEQ], ACT.Copy).then_inc(sem("kr_ev"), 1)

        def conv_first(it, tiles, banks):
            for t, b in zip(tiles, banks):
                S.activation(xs[:, t, :], bank(b)[:, 0:SEQ], ACT.Identity,
                                 scale=gp_main[:, 18 + t:19 + t], bias=gp_main[:, 24 + t:25 + t]) \
                                     .then_inc(sem("conv_acc"), 1)

        def ssm_main(it, c_):
            head = isinstance(it, int)
            if c_ == 6:
                group_end("ssm", it, 3)
                act.wait_ge(sem("gpm"), it + 1)
                if not head:
                    act.wait_ge(sem("cb_mm"), it)
                conv_first(it, (4, 5), (4, 5))
            if c_ in (10, 14):
                i = (c_ - 10) // 4
                group_end("ssm", it, 7 + 4 * i)
                if not head:
                    act.wait_ge(sem("y_skip"), it * 4 + (2 * i - 2))
                conv_first(it, (2 * i, 2 * i + 1), (2 * i, 2 * i + 1))
            if c_ == 19:
                act.wait_ge(sem("conv_done"), it * 6 + 6)
                S.activation(xs[:, :, :], xs[:, :, :], ACT.Silu).then_inc(sem("xs_act"), 1)

        def ssm_side(it, c_):
            if c_ == 2:
                group_end("ssm", it - 1, 19)
                act.wait_ge(sem("ssm_lo"), it - 1 + CREDIT["ssm_lo"])
                S.activation(z[:, :, :], psum[:, 0:4, 0:SEQ], ACT.Silu).then_inc(sem("z_act"), 1)
            if c_ in (5, 6, 9, 11):
                p = (5, 6, 9, 11).index(c_)
                for hd in (2 * p, 2 * p + 1):
                    act.wait_ge(sem("seg"), it * 16 - 16 + 2 * hd + 2)
                    S.activation(e[:, hd % 4, :], e[:, hd % 4, :], ACT.Exp).then_inc(sem("decay"), 1)
            if c_ == 14:
                act.wait_ge(sem("yz"), it * 4)
                S.activation(sq[:, :, :], z[:, :, :], ACT.Square).then_inc(sem("sq_ready"), 1)
            if c_ == 18:
                act.wait_ge(sem("ms"), it)
                S.activation(rs[:, 1, :], rs[:, 0, :], ACT.Ln).then_inc(sem("ln"), 1)
                act.wait_ge(sem("ln"), it)
                S.activation(rs[:, 1, :], rs[:, 1, :], ACT.Exp, scale=-0.5).then_inc(sem("r0"), 1)
                act.wait_ge(sem("yn"), it * 4)
                S.activation(g[:, bass.ds(it * 4 - 4, 4), 0, :], z[:, :, :], ACT.Copy).then_inc(sem("ssm_hi"), 1)

        for c_ in range(20):
            split("ssm", 0, c_)
            if c_ == 2:
                act.wait_ge(sem("dt_xb"), 2)
                S.activation(d_e[:, :, :], d_xb[:, :, :], ACT.Abs).then_inc(sem("dt_abs"), 1)
                act.wait_ge(sem("heads_in"), 48)
                S.activation(alog[:, :], alog[:, :], ACT.Exp).then_inc(sem("a_exp"), 1)
                act.wait_ge(sem("dt_abs"), 1)
                S.activation(d_e[:, :, :], d_e[:, :, :], ACT.Exp, scale=-1.0).then_inc(sem("dt_exp"), 1)
            if c_ == 15:
                act.wait_ge(sem("cum_mm"), 2)
                S.activation(cumt[:, :], bank(7)[0:64, 0:SEQ], ACT.Copy).then_inc(sem("cumt_ev"), 1)
            ssm_main(0, c_)
        with act.Fori(1, GROUPS) as it:
            for c_ in range(20):
                split("ssm", it, c_)
                ssm_side(it, c_)
                ssm_main(it, c_)

        def split_c(q):
            group_end("cq", 0, 4 * q + 3)
            b = (4, 0, 2, 4)[q]
            for i in range(2):
                t = 2 * q + i
                col = (V_QN if t < 4 else V_KVN) + t % 4
                S.activation(c[:, t, 0, :], bank(b + i)[:, 0:SEQ], ACT.Identity, scale=pv[:, col:col + 1]) \
                    .then_inc(sem("c_hi"), 1)
            if q:
                act.wait_ge(sem("accq"), ACCQ[q])
            S.activation(sqc, psum[:, b:b + 2, 0:SEQ], ACT.Square).then_inc(sem("c_sq"), 1)

        for c_ in range(20):
            split(*(("cq", 0, c_) if c_ < 16 else ("so", 0, c_ - 16)))
            ssm_side(GROUPS, c_)
            if c_ in (6, 10, 14, 19):
                split_c((6, 10, 14, 19).index(c_))

        def so_gate(it):
            group_end("so", it, 3)
            act.wait_ge(sem("so_ev"), it + CREDIT["so_ev"])
            S.activation(sg[:, :, :], psum[:, 0:2, 0:SEQ], ACT.Sigmoid).then_inc(sem("sg_so"), 1)

        for c_ in range(4, 12):
            split("so", 0, c_)
            if c_ == 5:
                for k, r in ((0, r_q), (1, r_kv)):
                    act.wait_ge(sem("qkv_ms"), k + 1)
                    S.activation(r, rs[:, k, :], ACT.Ln).then_inc(sem("qkv_ln"), 1)
                for k, r in ((0, r_q), (1, r_kv)):
                    act.wait_ge(sem("qkv_ln"), k + 1)
                    S.activation(r, r, ACT.Exp, scale=-0.5).then_inc(sem("qkv_r0"), 1)
            if c_ == 6:
                act.wait_ge(sem("ssm_lo"), GROUPS + CREDIT["ssm_lo"])
                so_gate(0)
            if c_ == 9:
                act.wait_ge(sem("angles"), 2)
                S.activation(sin[:, :], a_s[:, :], ACT.Sin).then_inc(sem("rope_sin"), 1)
                S.activation(cos[:, :], a_c[:, :], ACT.Sin).then_inc(sem("rope_tab"), 1)
        with act.Fori(1, 8) as it:
            for c_ in range(12):
                split("so", it, c_)
                if c_ == 6:
                    so_gate(it)

        def attn_side(it, c_):
            later = not (isinstance(it, int) and it == 1)
            if c_ == 0 and later:
                for hd in range(2):
                    act.wait_ge(sem("pt_mm"), it * 2 - 3 + hd)
                    if hd == 0 and not (isinstance(it, int) and it == 2):
                        act.wait_ge(sem("av_mm"), it - 2)
                    S.activation(pt[:, hd, :], bank(6 + hd)[:, 0:384], ACT.Copy).then_inc(sem("pt_ev"), 1)
            if c_ == 1 and later:
                act.wait_ge(sem("av_mm"), it - 1)
                S.activation(g[:, bass.ds(it * 2 - 4, 2), 0, :], bank(7).rearrange("p (a s) -> p a s", a=2),
                             ACT.Copy).then_inc(sem("o_hi"), 1)
            if c_ == 3 and not (isinstance(it, int) and it > 8):
                for hd in range(2):
                    for q, o, n in ((0, 0, 128), (1, 128, 256)):
                        act.wait_ge(sem("smax"), it * 2 - 1 + hd)
                        S.activation(sc[:, hd, o:o + n], sc[:, hd, o:o + n], ACT.Exp,
                                     bias=nm[:, hd, q:q + 1], scale=SCALE,
                                     accum_out=ls[:, hd, q:q + 1]).then_inc(sem("pexp"), 1)

        for c_ in range(4):
            split("at", 0, c_)
        for c_ in range(4):
            split("at", 1, c_)
            attn_side(1, c_)
        with act.Fori(2, 8) as it:
            for c_ in range(4):
                split("at", it, c_)
                attn_side(it, c_)

        def ao_gate(it):
            group_end("ao", it, 3)
            act.wait_ge(sem("ao_ev"), it + CREDIT["ao_ev"])
            S.activation(sg[:, :, :], psum[:, 0:2, 0:SEQ], ACT.Sigmoid).then_inc(sem("sg_ao"), 1)

        def ao_hi(it):
            act.wait_ge(sem("mixed"), it)
            S.activation(g[:, bass.ds(it * 2 + 14, 2), 0, :], prod[:, :, :], ACT.Copy).then_inc(sem("ao_hi"), 1)

        for c_ in range(8):
            split("ao", 0, c_)
            if c_ < 4:
                attn_side(8, c_)
            if c_ == 4:
                attn_side(9, 0)
            if c_ == 5:
                attn_side(9, 1)
            if c_ == 6:
                ao_gate(0)
        with act.Fori(1, 8) as it:
            for c_ in range(8):
                split("ao", it, c_)
                if c_ == 3:
                    ao_hi(it)
                if c_ == 6:
                    ao_gate(it)

        def sums_out(phase, k, last_chunk, src_banks, dst, sq_t, tile):
            group_end(phase, *last_chunk)
            act.wait_ge(sem(phase + "_acc"), k + CREDIT[phase + "_acc"])
            S.activation(sq_t, psum[:, src_banks:src_banks + 2, 0:SEQ], ACT.Square) \
                .then_inc(sem(phase + "_sq"), 1)
            S.activation(m[:, bass.ds(tile, 2), :], psum[:, src_banks:src_banks + 2, 0:SEQ], ACT.Copy) \
                .then_inc(sem(phase + "_cp"), 1)

        def wo_side(it, c_):
            if c_ == 6:
                sums_out("wo", it * 2, (it, 3), 0, m, sq_n[:, 0, :, :], it * 4)
            if c_ == 2 and not (isinstance(it, int) and it == 0):
                sums_out("wo", it * 2 - 1, (it - 1, 7), 2, m, sq_n[:, 0, :, :], it * 4 - 2)

        def h_copy(n):
            act.wait_ge(sem("ht_mm"), n + 1)
            b = (4, 5, 6, 7)[n % 4]
            S.activation(h[:, 2 * n:2 * n + 2, :], bank(b)[:, :], ACT.Copy).then_inc(sem("h_ev"), 1)

        for c_ in range(8):
            split("wo", 0, c_)
            if c_ == 3:
                ao_hi(8)
            wo_side(0, c_)
        with act.Fori(1, 4) as it:
            for c_ in range(8):
                split("wo", it, c_)
                wo_side(it, c_)
        for c_ in range(4):
            split("ff", 0, c_)
            wo_side(4, c_) if c_ == 2 else None
            if c_ == 0:
                for n in range(4):
                    h_copy(n)
            if c_ == 1:
                for n in range(4, 8):
                    h_copy(n)

        def residual(step, w, extra=None):
            for j in range(8):
                if extra:
                    extra(j)
                act.wait_ge(sem("h_new"), 8 * step + j + 1)
                for k in range(2):
                    kt = 2 * j + k
                    S.activation(u[:, kt, 0, :], h[:, kt, :], ACT.Identity, scale=pv[:, w + kt:w + kt + 1]) \
                        .then_inc(sem("u_hi"), 1)
                if 8 * step + j >= 2:
                    act.wait_ge(sem("hss_mm"), 8 * step + j - 1)
                S.activation(sq_n[:, j % 2, :, :], h[:, 2 * j:2 * j + 2, :], ACT.Square).then_inc(sem("hsq"), 1)

        rstd(keep[:, 0, :], keep[:, 1, :], "tot", 1)

        def next_gate(j):
            if 3 <= j < 7:
                split("ff", 0, j + 1)
        residual(0, V_FFPRE, next_gate)

        def gate_half(it, c_last, b):
            group_end("ff", it, c_last)
            S.activation(gx[:, :, :], psum[:, b:b + 2, SEQ:2 * SEQ], ACT.Copy).then_inc(sem("gx_cp"), 1)

        def gate_act(it):
            act.wait_ge(sem("ffg_norm"), it + 1)
            S.activation(fg[:, :, :], fg[:, :, :], ACT.Silu).then_inc(sem("ff_act"), 1)

        def ff_side(it, c_):
            if c_ == 2:
                group_end("ff", it - 1, 7)
                S.activation(ux[:, :, :], psum[:, 2:4, SEQ:2 * SEQ], ACT.Copy).then_inc(sem("ux_cp"), 1)
            if c_ == 3:
                act.wait_ge(sem("ff_prod"), it)
                S.activation(g[:, bass.ds(it * 2 - 2, 2), 0, :], fu[:, :, :], ACT.Copy).then_inc(sem("ff_hi"), 1)
            if c_ == 6:
                gate_half(it, 3, 0)
            if c_ == 7:
                gate_act(it)

        for c_ in range(8):
            split("ff", 1, c_)
            if c_ == 0:
                rstd(keep[:, 0, :], keep[:, 1, :], "hn", 1)
                gate_half(0, 6, 4)
            if c_ == 1:
                gate_act(0)
            ff_side(1, c_)
        with act.Fori(2, 22) as it:
            for c_ in range(8):
                split("ff", it, c_)
                ff_side(it, c_)

        def dn_half(k, last_chunk, b):
            group_end("dn", *last_chunk)
            S.activation(dx[:, :, :], psum[:, b:b + 2, SEQ:2 * SEQ], ACT.Copy).then_inc(sem("dx_cp"), 1)

        def dn_square(k, tile):
            act.wait_ge(sem("dn_acc"), k + CREDIT["dn_acc"])
            act.wait_ge(sem("dn_cp"), k + 1 + CREDIT["dn_cp"])
            S.activation(sq_d[:, :, :], m[:, bass.ds(tile, 2), :], ACT.Square).then_inc(sem("dn_sq"), 1)

        def dn_side(it, c_):
            later = not (isinstance(it, int) and it == 0)
            if c_ == 14:
                dn_half(it * 2, (it, 11), 0)
            if c_ == 15:
                dn_square(it * 2, it * 4)
            if c_ == 2 and later:
                dn_half(it * 2 - 1, (it - 1, 23), 2)
            if c_ == 3 and later:
                dn_square(it * 2 - 1, it * 4 - 2)

        for c_ in range(24):
            split("dn", 0, c_)
            if c_ in (2, 3):
                ff_side(22, c_)
            dn_side(0, c_)
            if c_ == 16:
                act.wait_ge(sem("pt8_mm"), 1)
                S.activation(pc[:, :, 0, :], bank(4)[:, :].rearrange("p (k s) -> p k s", k=2), ACT.Copy) \
                    .then_inc(sem("pc_hi"), 1)
        with act.Fori(1, 4) as it:
            for c_ in range(24):
                split("dn", it, c_)
                dn_side(it, c_)

        for c_ in range(4):
            split("pl", 0, c_)
            if c_ == 2:
                dn_side(4, 2)
                dn_side(4, 3)

        def ee_out(n):
            act.wait_ge(sem("chunk_done"), BASE["pl"] + n + 1)
            S.activation(ee[:, 4 * n:4 * n + 4, :], psum[:, 4:8, 0:SEQ], ACT.Copy).then_inc(sem("ee_ev"), 1)

        def between(j):
            if j in (1, 2):
                ee_out(j + 1)
            split("pg", 0, j)
            if j == 6:
                act.wait_ge(sem("chunk_done"), BASE["pg"])
        ee_out(0)
        rstd(keep[:, 0, :], keep[:, 1, :], "tot", 2)
        ee_out(1)
        residual(1, V_PLPRE, between)

        def pg_side(k, last_chunk, b, c_, tile):
            if c_ == 0:
                act.wait_ge(sem("pg_ev"), k + 1 + CREDIT["pg_ev"])
                S.activation(ga[:, :, :], ga[:, :, :], ACT.Sigmoid).then_inc(sem("pg_act"), 1)
            else:
                act.wait_ge(sem("pg_e"), k + 1)
                act.wait_ge(sem("pg_acc"), k + CREDIT["pg_acc"])
                S.activation(sq_n[:, 0, :, :], ee[:, bass.ds(tile, 2), :], ACT.Square).then_inc(sem("pg_sq"), 1)

        def pg_iter(it, c_):
            if c_ in (6, 7):
                pg_side(it * 2, (it, 3), 0, c_ - 6, it * 4)
            if c_ in (2, 3) and not (isinstance(it, int) and it == 0):
                pg_side(it * 2 - 1, (it - 1, 7), 2, c_ - 2, it * 4 - 2)

        for c_ in range(8):
            split("pg", 1, c_)
            if c_ == 0:
                rstd(keep[:, 0, :], keep[:, 1, :], "hn", 2)
            if c_ in (0, 1):
                pg_iter(0, c_ + 6)
            pg_iter(1, c_)
        with act.Fori(2, 4) as it:
            for c_ in range(8):
                split("pg", it, c_)
                pg_iter(it, c_)
        pg_iter(4, 2)
        pg_iter(4, 3)
        rstd(keep[:, 0, :], keep[:, 1, :], "tot", 3)
        for j in range(8):
            act.wait_ge(sem("ot_mm"), j + 1)
            S.activation(ot[:, :, 2 * j * P:2 * j * P + 2 * P],
                             bank(j)[:, :].rearrange("p (b n) -> p b n", b=2), ACT.Copy) \
                                 .then_inc(sem("ot_ready"), 1)

    @block.vector
    def _(dve):
        def split(phase, it, c):
            slot, w = c % RING, width(phase, c)
            dve.wait_ge(sem("hi_ready"), num(phase, it, c) + 1)
            V.tensor_tensor(wlo[:, slot, 0:w], raw[:, slot, 0:w], whi[:, slot, 0:w].bitcast(F32), ALU.subtract) \
                .then_inc(sem("lo_ready"), 1)

        def group_end(phase, it, c_last):
            dve.wait_ge(sem("chunk_done"), num(phase, it, c_last) + 1)

        def both(r):
            return r.unsqueeze(1).to_broadcast([P, 2, SEQ])

        steps = [0]

        def link(ins):
            steps[0] += 1
            ins.then_inc(sem("dve_step"), 1)
            dve.wait_ge(sem("dve_step"), steps[0])

        def newton(ms, r0, tmp, final, dst=None):
            link(V.tensor_tensor(tmp, r0, r0, ALU.mult))
            link(V.scalar_tensor_tensor(tmp, tmp, -0.5, ms, ALU.mult, ALU.mult))
            ins = V.scalar_tensor_tensor(tmp if dst is None else dst, tmp, 1.5, r0, ALU.add, ALU.mult)
            if final:
                ins.then_inc(sem(final), 1)
            else:
                link(ins)

        dve.wait_ge(sem("x_ssq"), 2)
        V.tensor_scalar(st0[:, 2:4], st0[:, 0:2], 1.0 / D_MODEL, EPS, ALU.mult, ALU.add).then_inc(sem("x_ms"), 1)
        dve.wait_ge(sem("x_r0"), 1)
        newton(st0[:, 2:4], st0[:, 4:6], st0[:, 6:8], None)
        for b in range(2):
            V.tensor_scalar(xn_tok[:, b, :], x_tok[:, b, :], st0[:, 6 + b:7 + b], None, ALU.mult) \
                .then_inc(sem("xn_ready"), 1)
        dve.wait_ge(sem("pv_mm"), 1)
        V.tensor_copy(pv_all[:, :], bank(7)[:, 0:V_ALL]).then_inc(sem("pv_ev"), 1)
        dve.wait_ge(sem("pv_ev"), 1)
        V.tensor_copy(pv[:, :], pv_all[:, 0:V_KEEP]).then_inc(sem("pv_kept"), 1)
        for b in range(8):
            dve.wait_ge(sem("u_hi"), 2 * b + 2)
            for k in range(2):
                kt = 2 * b + k
                V.scalar_tensor_tensor(u[:, kt, 1, :], bank(b)[:, k * SEQ:k * SEQ + SEQ],
                                           pv_all[:, V_MIXPRE + kt:V_MIXPRE + kt + 1],
                                           u[:, kt, 0, :].bitcast(F32), ALU.mult, ALU.subtract) \
                                               .then_inc(sem("u_lo"), 1)
            if b in (2, 4, 6, 7):
                split("kr", 0, (2, 4, 6, 7).index(b))

        link(V.memset(xdt[:, :, :, 64:128], 0.0))
        taps = pv_all[:, V_TAP:V_ALL].rearrange("p (a n) -> p a n", a=4)
        gp_taps = gp_all[:, :, 0:24].rearrange("p g (a t) -> p a g t", t=6)
        V.tensor_copy(gp_taps[:, :, :, 0:4], taps[:, :, 0:32].rearrange("p a (g t) -> p a g t", t=4))
        for i in range(2):
            V.tensor_copy(gp_taps[:, :, :, 4 + i], taps[:, :, 32 + 8 * i:40 + 8 * i])
        V.tensor_copy(gp_all[:, :, 24:28], pv_all[:, V_CB:V_CB + 32].rearrange("p (g t) -> p g t", t=4))
        for i in range(2):
            V.tensor_copy(gp_all[:, :, 28 + i], pv_all[:, V_CB + 32 + 8 * i:V_CB + 40 + 8 * i])
        V.tensor_copy(gp_all[:, :, 30:34], pv_all[:, V_SN:V_SN + 32].rearrange("p (g t) -> p g t", t=4))
        dve.wait_ge(sem("heads_in"), 48)
        for i in range(2):
            half = slice(64 * i, 64 * i + 64)
            last = V.tensor_copy(gp_all[half, :, 34:38],
                                 dsk[half, :].rearrange("p (g t i) -> p g t i", t=4, i=2)[:, :, :, i])
            if i == 0:
                link(last)
        last.then_inc(sem("gp_all"), 1)
        dve.wait_ge(sem("gp_all"), 1)
        def prepare_dt():
            dve.wait_ge(sem("dt_mm"), 1)
            for blk in range(2):
                V.tensor_tensor(d_xb[:, blk, :], bank(1 + blk)[:, 0:64], dtb[:, :], ALU.add) \
                    .then_inc(sem("dt_xb"), 1)

        def softplus():
            dve.wait_ge(sem("dt_exp"), 1)
            link(V.tensor_scalar(d_r[:, :, :], d_e[:, :, :], 2.0, None, ALU.add))
            link(V.reciprocal(d_r[:, :, :], d_r[:, :, :]))
            link(V.tensor_tensor(d_s[:, :, :], d_e[:, :, :], d_r[:, :, :], ALU.mult))
            link(V.tensor_tensor(d_s2[:, :, :], d_s[:, :, :], d_s[:, :, :], ALU.mult))
            link(V.tensor_scalar(d_q[:, :, :], d_s2[:, :, :], 2.0 / 15, None, ALU.mult))
            for k in (13, 11, 9, 7, 5, 3):
                link(V.scalar_tensor_tensor(d_q[:, :, :], d_q[:, :, :], 2.0 / k, d_s2[:, :, :], ALU.add, ALU.mult))
            link(V.scalar_tensor_tensor(d_q[:, :, :], d_q[:, :, :], 2.0, d_s[:, :, :], ALU.add, ALU.mult))
            link(V.scalar_tensor_tensor(dt_tok[:, :, :], d_xb[:, :, :], 0.0, d_q[:, :, :], ALU.max, ALU.add))
            dve.wait_ge(sem("a_exp"), 1)
            V.scalar_tensor_tensor(da[:, :, :], dt_tok[:, :, :], -1.0,
                                       alog[:, :].unsqueeze(1).to_broadcast([P, 2, HEADS_SSM]),
                                       ALU.mult, ALU.mult).then_inc(sem("da_ready"), 1)

        def conv_rest(it, pair, tiles, banks):
            for k, a in enumerate((2, 1, 0)):
                for i, (t, b) in enumerate(zip(tiles, banks)):
                    if k == 0:
                        dve.wait_ge(sem("conv_acc"), it * 6 + (2 * pair + i + 1))
                    else:
                        dve.wait_ge(sem("conv_tap"), it * 12 + (4 * pair + 2 * (k - 1) + i + 1))
                    sh = 3 - a
                    ins = V.scalar_tensor_tensor(xs[:, t, sh:SEQ], bank(b)[:, 0:SEQ - sh],
                                                 gp_main[:, 6 * a + t:6 * a + t + 1], xs[:, t, sh:SEQ],
                                                 ALU.mult, ALU.add)
                    ins.then_inc(sem("conv_done" if k == 2 else "conv_tap"), 1)

        def ssm_main(it, c_):
            if c_ == 0:
                if not isinstance(it, int):
                    dve.wait_ge(sem("conv_acc"), it * 6)
                V.tensor_copy(gp_main[:, :], gp_all[:, bass.ds(it, 1), 0:30].rearrange("p a n -> p (a n)")) \
                    .then_inc(sem("gpm"), 1)
                dve.wait_ge(sem("gpm"), it + 1)
            if c_ == 7:
                conv_rest(it, 0, (4, 5), (4, 5))
            if c_ == 11:
                conv_rest(it, 1, (0, 1), (0, 1))
            if c_ == 15:
                conv_rest(it, 2, (2, 3), (2, 3))

        def decays(it, p):
            for hd in (2 * p, 2 * p + 1):
                if hd >= 4:
                    dve.wait_ge(sem("y_mm"), it * 4 - 4 + (hd - 4) // 2 + 1)
                for blk, o, n in ((0, 0, 256), (1, 256, 128)):
                    V.tensor_scalar(e[:, hd % 4, o:o + n], cumb[:, hd, SEQ - n:SEQ], cum_g[:, blk, hd:hd + 1],
                                        0.0, ALU.subtract, ALU.min).then_inc(sem("seg"), 1)

        def mask_scores(it, p):
            for hd in (2 * p, 2 * p + 1):
                dve.wait_ge(sem("decay"), it * 8 - 8 + hd + 1)
                V.tensor_tensor(e[:, hd % 4, :], e[:, hd % 4, :], cbm[:, :], ALU.mult).then_inc(sem("masked"), 1)

        def x_dt(it, blk):
            dve.wait_ge(sem("xtr_mm"), it * 2 - 1 + blk)
            V.tensor_tensor(xdt[:, blk, :, :].rearrange("p q (a n) -> p q a n", a=3)[:, :, 0:3:2, :],
                                bank(7 - blk)[:, :].rearrange("p (q a n) -> p q a n", q=4, a=2),
                                dt_g[:, blk, :].rearrange("p (q a) -> p q a", a=2).unsqueeze(3)
                                .to_broadcast([P, 4, 2, PDIM]), ALU.mult).then_inc(sem("xdt_ready"), 1)

        def y_gate(it, p):
            dve.wait_ge(sem("y_mm"), it * 4 - 3 + p)
            if p == 0:
                dve.wait_ge(sem("z_act"), it)
            V.scalar_tensor_tensor(yb[:, p % 2, :], xs[:, p, :], gp_side[:, 4 + p:5 + p],
                                       bank(7 - p % 2)[:, 0:SEQ], ALU.mult, ALU.add).then_inc(sem("y_skip"), 1)
            dve.wait_ge(sem("y_skip"), it * 4 - 3 + p)
            V.tensor_tensor(z[:, p, :], z[:, p, :], yb[:, p % 2, :], ALU.mult).then_inc(sem("yz"), 1)

        def ssm_side(it, c_):
            if c_ == 3:
                V.tensor_copy(gp_side[:, :], gp_all[:, bass.ds(it - 1, 1), 30:38]
                                  .rearrange("p a n -> p (a n)")).then_inc(sem("gps"), 1)
                hh = bass.ds(it * HPG - HPG, HPG)
                V.tensor_copy(cum_g[:, :, :], cum_tok[:, :, hh]).then_inc(sem("gps"), 1)
                V.tensor_copy(dt_g[:, :, :], dt_tok[:, :, hh]).then_inc(sem("gps"), 1)
                dve.wait_ge(sem("cb_mm"), it)
                diag = cbm[:, :].rearrange("p (q n) -> p q n", q=3)
                V.tensor_tensor(diag[:, 0:3:2, :],
                                    bank(6)[:, 0:384].rearrange("p (q n) -> p q n", q=3)[:, 0:3:2, :],
                                    tri.unsqueeze(1).to_broadcast([P, 2, P]), ALU.mult).then_inc(sem("cbd"), 1)
                V.tensor_copy(diag[:, 1, :], bank(6)[:, 128:256]).then_inc(sem("cbm_ev"), 1)
                dve.wait_ge(sem("gps"), it * 3)
                x_dt(it, 0)
            if c_ == 4:
                dve.wait_ge(sem("cumb_in"), it * 16)
                decays(it, 0)
            if c_ == 5:
                dve.wait_ge(sem("cbm_ev"), it)
                mask_scores(it, 0)
                decays(it, 1)
            if c_ == 6:
                x_dt(it, 1)
                mask_scores(it, 1)
            if c_ == 8:
                y_gate(it, 0)
                decays(it, 2)
            if c_ == 9:
                mask_scores(it, 2)
            if c_ == 10:
                y_gate(it, 1)
                decays(it, 3)
            if c_ == 11:
                mask_scores(it, 3)
            if c_ == 12:
                y_gate(it, 2)
            if c_ == 14:
                y_gate(it, 3)
            if c_ == 17:
                dve.wait_ge(sem("ss_mm"), it)
                V.tensor_scalar(rs[:, 0, :], bank(7)[:, 0:SEQ], 1.0 / 512, EPS, ALU.mult, ALU.add) \
                    .then_inc(sem("ms"), 1)
            if c_ == 18:
                dve.wait_ge(sem("r0"), it)
                V.tensor_tensor(rs[:, 2, :], rs[:, 1, :], rs[:, 1, :], ALU.mult).then_inc(sem("nt"), 1)
                dve.wait_ge(sem("nt"), it * 3 - 2)
                V.scalar_tensor_tensor(rs[:, 2, :], rs[:, 2, :], -0.5, rs[:, 0, :], ALU.mult, ALU.mult) \
                    .then_inc(sem("nt"), 1)
                dve.wait_ge(sem("nt"), it * 3 - 1)
                V.scalar_tensor_tensor(rs[:, 2, :], rs[:, 2, :], 1.5, rs[:, 1, :], ALU.add, ALU.mult) \
                    .then_inc(sem("nt"), 1)
                dve.wait_ge(sem("nt"), it * 3)
                for t in range(4):
                    V.scalar_tensor_tensor(z[:, t, :], z[:, t, :], gp_side[:, t:t + 1], rs[:, 2, :],
                                               ALU.mult, ALU.mult).then_inc(sem("yn"), 1)
            if c_ == 19:
                dve.wait_ge(sem("ssm_hi"), it)
                tiles = bass.ds(it * 4 - 4, 4)
                V.tensor_tensor(g[:, tiles, 1, :], z[:, :, :], g[:, tiles, 0, :].bitcast(F32), ALU.subtract) \
                    .then_inc(sem("ssm_lo"), 1)

        for c_ in range(20):
            split("ssm", 0, c_)
            if c_ == 1:
                prepare_dt()
            if c_ == 4:
                softplus()
            ssm_main(0, c_)
            if c_ == 15:
                dve.wait_ge(sem("cum_mm"), 1)
                V.tensor_copy(cum_tok[:, :, :].rearrange("p b h -> p (b h)"), bank(6)[:, 0:128]) \
                    .then_inc(sem("cum_ev"), 1)
                dve.wait_ge(sem("cumt_ev"), 1)
        with dve.Fori(1, GROUPS) as it:
            for c_ in range(20):
                split("ssm", it, c_)
                ssm_side(it, c_)
                ssm_main(it, c_)

        def split_c(q):
            b = (4, 0, 2, 4)[q]
            dve.wait_ge(sem("c_sq"), q + 1)
            for i in range(2):
                t = 2 * q + i
                col = (V_QN if t < 4 else V_KVN) + t % 4
                V.scalar_tensor_tensor(c[:, t, 1, :], bank(b + i)[:, 0:SEQ], pv[:, col:col + 1],
                                           c[:, t, 0, :].bitcast(F32), ALU.mult, ALU.subtract) \
                                               .then_inc(sem("c_lo"), 1)
            acc = acc_q[:, q // 2, :]
            if q % 2 == 0:
                V.tensor_tensor(acc, sqc[:, 0, :], sqc[:, 1, :], ALU.add).then_inc(sem("accq"), 1)
            else:
                V.tensor_tensor(acc, acc, sqc[:, 0, :], ALU.add).then_inc(sem("accq"), 1)
                dve.wait_ge(sem("accq"), ACCQ[q] + 1)
                V.tensor_tensor(acc, acc, sqc[:, 1, :], ALU.add).then_inc(sem("accq"), 1)

        for c_ in range(20):
            split(*(("cq", 0, c_) if c_ < 16 else ("so", 0, c_ - 16)))
            ssm_side(GROUPS, c_)
            if c_ in (7, 11, 15, 19):
                split_c((7, 11, 15, 19).index(c_))

        def so_evac(it):
            group_end("so", it, 11)
            dve.wait_ge(sem("sg_so"), it + 1 + CREDIT["sg_so"])
            V.tensor_tensor(m[:, bass.ds(it * 2, 2), :], psum[:, 2:4, 0:SEQ], sg[:, :, :], ALU.mult) \
                .then_inc(sem("so_ev"), 1)

        TWO_PI = 2.0 * np.pi
        C1 = 6.28125
        C2 = float(np.float32(round((TWO_PI - C1) * 2.0 ** 22) / 2.0 ** 22))
        C3 = TWO_PI - C1 - C2
        ROUND = 1.5 * 2.0 ** 23

        def angle(dst, turn):
            link(V.tensor_scalar(a_k[:, :], a_ang[:, :], 1.0 / TWO_PI, turn, ALU.mult, ALU.add))
            link(V.tensor_scalar(a_k[:, :], a_k[:, :], ROUND, ROUND, ALU.add, ALU.subtract))
            link(V.scalar_tensor_tensor(dst, a_k[:, :], -C1, a_ang[:, :], ALU.mult, ALU.add))
            link(V.scalar_tensor_tensor(dst, a_k[:, :], -C2, dst, ALU.mult, ALU.add))
            link(V.scalar_tensor_tensor(dst, a_k[:, :], -C3, dst, ALU.mult, ALU.add))
            if turn:
                link(V.tensor_scalar(dst, dst, turn * TWO_PI, None, ALU.add))
            V.tensor_scalar(dst, dst, 3.1415925, -3.1415925, ALU.min, ALU.max).then_inc(sem("angles"), 1)

        for c_ in range(4, 12):
            split("so", 0, c_)
            if c_ == 4:
                for k in range(2):
                    dve.wait_ge(sem("ssqkv_mm"), k + 1)
                    V.tensor_scalar(rs[:, k, :], bank(6 + k)[:, 0:SEQ], 1.0 / Q_LORA, EPS, ALU.mult, ALU.add) \
                        .then_inc(sem("qkv_ms"), 1)
            if c_ == 5:
                for k, r in ((0, r_q), (1, r_kv)):
                    dve.wait_ge(sem("qkv_r0"), k + 1)
                    newton(rs[:, k, :], r, rs[:, 2, :], "rkv_ready" if k else None, dst=r)
                dve.wait_ge(sem("rkv_ready"), 1)
            if c_ == 6:
                dve.wait_ge(sem("pos_in"), 16)
                dve.wait_ge(sem("rope_in"), 16)
                link(V.tensor_copy(a_k[:, :], pos_i[:, :]))
                link(V.tensor_scalar(a_ang[:, :], a_k[:, :], invf, None, ALU.mult))
                angle(a_s[:, :], 0.0)
            if c_ == 7:
                dve.wait_ge(sem("angles"), 1)
                angle(a_c[:, :], 0.25)
        with dve.Fori(1, 8) as it:
            for c_ in range(12):
                split("so", it, c_)
                if c_ == 2:
                    so_evac(it - 1)

        def attn_rest(it):
            dve.wait_ge(sem("o_hi"), it - 1)
            tiles = bass.ds(it * 2 - 4, 2)
            V.tensor_tensor(g[:, tiles, 1, :], bank(7).rearrange("p (a s) -> p a s", a=2),
                            g[:, tiles, 0, :].bitcast(F32), ALU.subtract).then_inc(sem("o_lo"), 1)

        def keys(it):
            group_end("at", it - 1, 2)
            if not (isinstance(it, int) and it == 1):
                dve.wait_ge(sem("scores_mm"), it * 2 - 2)
            V.tensor_tensor(kn[:, :, :], bank(3).rearrange("p (a s) -> p a s", a=2), both(r_kv), ALU.mult) \
                .then_inc(sem("kn_ev"), 1)

        def values(it):
            group_end("at", it - 1, 3)
            if not (isinstance(it, int) and it == 1):
                dve.wait_ge(sem("av_mm"), it - 1)
            V.tensor_tensor(vt[:, :, :, :], bank(1).rearrange("p (b a n) -> p b a n", b=2, a=2),
                            rkv_tok[:, :].unsqueeze(2).unsqueeze(3).to_broadcast([P, 2, 2, VDIM]), ALU.mult) \
                .then_inc(sem("v_ev"), 1)

        def rotate(it):
            dve.wait_ge(sem("rot_mm"), it)
            V.tensor_tensor(rt[:, 0, :], qp[:, :], cos[:, :], ALU.mult).then_inc(sem("rope_t"), 1)
            V.tensor_tensor(rt[:, 1, :], bank(6)[:, 0:SEQ], sin[:, :], ALU.mult).then_inc(sem("rope_t"), 1)
            dve.wait_ge(sem("rope_t"), it * 2)
            if not (isinstance(it, int) and it == 1):
                dve.wait_ge(sem("scores_mm"), it * 2 - 2)
            for hd in range(2):
                half = slice(64 * hd, 64 * hd + 64)
                V.tensor_tensor(qr[half, hd, :], rt[half, 0, :], rt[half, 1, :], ALU.add) \
                    .then_inc(sem("rope_done"), 1)

        def attn_max(it):
            for hd in range(2):
                dve.wait_ge(sem("scores_mm"), it * 2 - 1 + hd)
                V.memset(pad[:, :], 0.0)
                for q, o, n in ((0, 0, 128), (1, 128, 256)):
                    V.tensor_tensor_reduce(out=sc[:, hd, o:o + n], in0=bank(4 + hd)[:, o:o + n],
                                               in1=mask_a[:, o:o + n], scale=1.0, scalar=-3.0e38,
                                               op0=ALU.add, op1=ALU.max, accum_out=mx[:, hd, q:q + 1]) \
                                                   .then_inc(sem("rowmax"), 1)
                dve.wait_ge(sem("rowmax"), it * 4 - 2 + 2 * hd)
                V.tensor_scalar(nm[:, hd, :], mx[:, hd, :], -SCALE, None, ALU.mult).then_inc(sem("smax"), 1)

        def attn_norm(it):
            for hd in range(2):
                dve.wait_ge(sem("pexp"), it * 4 - 2 + 2 * hd)
                V.reciprocal(rl[:, hd, :], ls[:, hd, :]).then_inc(sem("rsum"), 1)
                dve.wait_ge(sem("rsum"), it * 2 - 1 + hd)
                V.tensor_scalar(sc[:, hd, 0:128], sc[:, hd, 0:128], rl[:, hd, 0:1], None, ALU.mult)
                V.tensor_scalar(sc[:, hd, 128:384], sc[:, hd, 128:384], rl[:, hd, 1:2], None, ALU.mult) \
                    .then_inc(sem("pn"), 1)

        def queries(it):
            group_end("at", it, 1)
            if not (isinstance(it, int) and it == 0):
                dve.wait_ge(sem("scores_mm"), it * 2)
            V.tensor_tensor(qp[:, :], bank(2)[:, 0:SEQ], r_q, ALU.mult).then_inc(sem("qp_ev"), 1)
            V.tensor_tensor(qn[:, :, :], bank(0)[:, :].rearrange("p (a n) -> p a n", a=2), both(r_q), ALU.mult) \
                .then_inc(sem("q_ev"), 1)

        def attn_side(it, c_):
            if c_ == 0:
                keys(it)
            if c_ == 1:
                if isinstance(it, int) and it == 8:
                    values(it)
                    rotate(it)
                else:
                    rotate(it)
                    values(it)
            if c_ == 2:
                attn_max(it)
                if not (isinstance(it, int) and it == 1):
                    attn_rest(it)
            if c_ == 3:
                attn_norm(it)

        for c_ in range(4):
            split("at", 0, c_)
            if c_ == 0:
                dve.wait_ge(sem("rope_tab"), 1)
                dve.wait_ge(sem("krot_mm"), 1)
                link(V.tensor_tensor(a_s[:, :], bank(4)[:, 0:SEQ], sin[:, :], ALU.mult))
                link(V.tensor_tensor(kpe[:, :], bank(4)[:, SEQ:2 * SEQ], cos[:, :], ALU.mult))
                link(V.tensor_tensor(kpe[:, :], kpe[:, :], a_s[:, :], ALU.add))
                link(V.memset(qr[:, :, :], 0.0))
                dve.wait_ge(sem("rkvt_mm"), 1)
                V.tensor_copy(rkv_tok[:, :], bank(5)[:, 0:256:128]).then_inc(sem("rkvt_ev"), 1)
            if c_ == 2:
                so_evac(7)
            if c_ == 3:
                queries(0)
        for c_ in range(4):
            split("at", 1, c_)
            attn_side(1, c_)
            if c_ == 3:
                queries(1)
        with dve.Fori(2, 8) as it:
            for c_ in range(4):
                split("at", it, c_)
                attn_side(it, c_)
                if c_ == 3:
                    queries(it)

        def ao_evac(it):
            group_end("ao", it, 7)
            dve.wait_ge(sem("sg_ao"), it + 1 + CREDIT["sg_ao"])
            V.tensor_tensor(prod[:, :, :], psum[:, 2:4, 0:SEQ], sg[:, :, :], ALU.mult).then_inc(sem("ao_ev"), 1)
            dve.wait_ge(sem("ao_ev"), it + 1 + CREDIT["ao_ev"])
            V.tensor_tensor(prod[:, :, :], prod[:, :, :], m[:, bass.ds(it * 2, 2), :], ALU.add) \
                .then_inc(sem("mixed"), 1)

        def ao_rest(it):
            dve.wait_ge(sem("ao_hi"), it + 1)
            tiles = bass.ds(it * 2 + 16, 2)
            V.tensor_tensor(g[:, tiles, 1, :], prod[:, :, :], g[:, tiles, 0, :].bitcast(F32), ALU.subtract) \
                .then_inc(sem("ao_lo"), 1)

        for c_ in range(8):
            split("ao", 0, c_)
            if c_ < 4:
                attn_side(8, c_)
            if c_ == 6:
                attn_rest(9)
        with dve.Fori(1, 8) as it:
            for c_ in range(8):
                split("ao", it, c_)
                if c_ == 2:
                    ao_evac(it - 1)
                if c_ == 3:
                    ao_rest(it - 1)

        def add_squares(phase, k, sq_t, acc):
            dve.wait_ge(sem(phase + "_sq"), k + 1)
            V.tensor_tensor(acc[:, :, :], acc[:, :, :], sq_t, ALU.add).then_inc(sem(phase + "_acc"), 1)

        def wo_side(it, c_):
            if c_ == 7:
                add_squares("wo", it * 2, sq_n[:, 0, :, :], acc_n)
            if c_ == 3 and not (isinstance(it, int) and it == 0):
                add_squares("wo", it * 2 - 1, sq_n[:, 0, :, :], acc_n)

        for c_ in range(8):
            split("wo", 0, c_)
            if c_ == 1:
                dve.wait_ge(sem("chunk_done"), BASE["wo"])
                link(V.memset(acc_n[:, :, :], 0.0))
            if c_ == 2:
                ao_evac(7)
            if c_ == 3:
                ao_rest(7)
            wo_side(0, c_)
        with dve.Fori(1, 4) as it:
            for c_ in range(8):
                split("wo", it, c_)
                wo_side(it, c_)
        for c_ in range(4):
            split("ff", 0, c_)

        def total(n, b):
            dve.wait_ge(sem("tot_mm"), n)
            V.tensor_scalar(keep[:, 0, :], bank(b)[:, 0:SEQ], 1.0 / D_MODEL, EPS, ALU.mult, ALU.add) \
                .then_inc(sem("tot_ms"), 1)
            dve.wait_ge(sem("tot_r0"), n)
            newton(keep[:, 0, :], keep[:, 1, :], keep[:, 2, :], None)

        def residual(step, src, w_post, w_next, extra=None):
            for j in range(8):
                if j == 0:
                    norm_part(step, src, w_post, 0)
                dve.wait_ge(sem("bt"), 16 * step + 2 * j + 2)
                V.tensor_tensor(h[:, 2 * j:2 * j + 2, :], h[:, 2 * j:2 * j + 2, :], bt[:, j % 2, :, :], ALU.add) \
                    .then_inc(sem("h_new"), 1)
                if j < 7:
                    norm_part(step, src, w_post, j + 1)
                if extra:
                    extra(j)
                if w_next is None:
                    continue
                dve.wait_ge(sem("u_hi"), KT * (step + 1) + 2 * j + 2)
                for k in range(2):
                    kt = 2 * j + k
                    V.scalar_tensor_tensor(u[:, kt, 1, :], h[:, kt, :], pv[:, w_next + kt:w_next + kt + 1],
                                           u[:, kt, 0, :].bitcast(F32), ALU.mult, ALU.subtract) \
                        .then_inc(sem("u_lo"), 1)

        def norm_part(step, src, w_post, j):
            if 8 * step + j - 1 > 0:
                dve.wait_ge(sem("h_new"), 8 * step + j - 1)
            for k in range(2):
                kt = 2 * j + k
                V.scalar_tensor_tensor(bt[:, j % 2, k, :], src[:, kt, :], pv[:, w_post + kt:w_post + kt + 1],
                                       keep[:, 2, :], ALU.mult, ALU.mult).then_inc(sem("bt"), 1)

        def hidden_norm(n):
            dve.wait_ge(sem("hss_mm"), 8 * n)
            V.tensor_scalar(keep[:, 0, :], bank(6)[:, 0:SEQ], 1.0 / D_MODEL, EPS, ALU.mult, ALU.add) \
                .then_inc(sem("hn_ms"), 1)
            dve.wait_ge(sem("hn_r0"), n)
            newton(keep[:, 0, :], keep[:, 1, :], keep[:, 2, :], None)

        dve.wait_ge(sem("h_ev"), 8)
        total(1, 7)
        dve.wait_ge(sem("wo_cp"), 8 + CREDIT["wo_cp"])

        def next_gate(j):
            if 3 <= j < 7:
                split("ff", 0, j + 1)
        residual(0, m, V_MIXPOST, V_FFPRE, next_gate)

        def gate_out(it, c_last, b):
            dve.wait_ge(sem("gx_cp"), it + 1)
            V.tensor_tensor(fg[:, :, :], psum[:, b:b + 2, 0:SEQ], gx[:, :, :], ALU.add).then_inc(sem("ffg_ev"), 1)
            dve.wait_ge(sem("ffg_ev"), it + 1 + CREDIT["ffg_ev"])
            V.tensor_tensor(fg[:, :, :], fg[:, :, :], both(keep[:, 2, :]), ALU.mult).then_inc(sem("ffg_norm"), 1)

        def ff_side(it, c_):
            if c_ == 6:
                gate_out(it, 3, 0)
            if c_ == 2:
                dve.wait_ge(sem("ux_cp"), it)
                V.tensor_tensor(fu[:, :, :], psum[:, 2:4, 0:SEQ], ux[:, :, :], ALU.add).then_inc(sem("ffu_ev"), 1)
                dve.wait_ge(sem("ffu_ev"), it + CREDIT["ffu_ev"])
                V.tensor_tensor(fu[:, :, :], fu[:, :, :], both(keep[:, 2, :]), ALU.mult).then_inc(sem("ffu_norm"), 1)
                dve.wait_ge(sem("ff_act"), it)
                dve.wait_ge(sem("ffu_norm"), it)
                V.tensor_tensor(fu[:, :, :], fu[:, :, :], fg[:, :, :], ALU.mult).then_inc(sem("ff_prod"), 1)
            if c_ == 3:
                dve.wait_ge(sem("ff_hi"), it)
                tiles = bass.ds(it * 2 - 2, 2)
                V.tensor_tensor(g[:, tiles, 1, :], fu[:, :, :], g[:, tiles, 0, :].bitcast(F32), ALU.subtract) \
                    .then_inc(sem("ff_lo"), 1)

        for c_ in range(8):
            split("ff", 1, c_)
            if c_ == 0:
                hidden_norm(1)
                gate_out(0, 6, 4)
            ff_side(1, c_)
        with dve.Fori(2, 22) as it:
            for c_ in range(8):
                split("ff", it, c_)
                ff_side(it, c_)

        def dn_out(k, b, tile):
            dve.wait_ge(sem("dx_cp"), k + 1)
            V.tensor_tensor(m[:, bass.ds(tile, 2), :], psum[:, b:b + 2, 0:SEQ], dx[:, :, :], ALU.add) \
                .then_inc(sem("dn_cp"), 1)

        def dn_side(it, c_):
            later = not (isinstance(it, int) and it == 0)
            if c_ == 14:
                dn_out(it * 2, 0, it * 4)
            if c_ == 16:
                add_squares("dn", it * 2, sq_d[:, :, :], acc_d)
            if c_ == 2 and later:
                dn_out(it * 2 - 1, 2, it * 4 - 2)
            if c_ == 4 and later:
                add_squares("dn", it * 2 - 1, sq_d[:, :, :], acc_d)

        for c_ in range(24):
            split("dn", 0, c_)
            if c_ in (2, 3):
                ff_side(22, c_)
            if c_ == 4:
                link(V.memset(acc_d[:, :, :], 0.0))
            dn_side(0, c_)
            if c_ == 17:
                dve.wait_ge(sem("pc_hi"), 1)
                V.tensor_tensor(pc[:, :, 1, :], bank(4)[:, :].rearrange("p (k s) -> p k s", k=2),
                                pc[:, :, 0, :].bitcast(F32), ALU.subtract).then_inc(sem("pc_lo"), 1)
        with dve.Fori(1, 4) as it:
            for c_ in range(24):
                split("dn", it, c_)
                dn_side(it, c_)
        for c_ in range(4):
            split("pl", 0, c_)
            if c_ == 2:
                dn_side(4, 2)
        total(2, 0)

        def between(j):
            split("pg", 0, j)
        residual(1, m, V_FFPOST, V_PLPRE, between)

        def pg_gate(k, last_chunk, b):
            group_end("pg", *last_chunk)
            V.tensor_tensor(ga[:, :, :], psum[:, b:b + 2, 0:SEQ], both(keep[:, 2, :]), ALU.mult) \
                .then_inc(sem("pg_ev"), 1)

        def pg_mul(k, tile):
            dve.wait_ge(sem("pg_act"), k + 1)
            tiles = bass.ds(tile, 2)
            V.tensor_tensor(ee[:, tiles, :], ee[:, tiles, :], ga[:, :, :], ALU.mult).then_inc(sem("pg_e"), 1)

        def pg_iter(it, c_):
            later = not (isinstance(it, int) and it == 0)
            if c_ == 6:
                pg_gate(it * 2, (it, 3), 0)
            if c_ == 7:
                pg_mul(it * 2, it * 4)
            if c_ == 0 and later:
                add_squares("pg", it * 2 - 2, sq_n[:, 0, :, :], acc_n)
            if c_ == 2 and later:
                pg_gate(it * 2 - 1, (it - 1, 7), 2)
            if c_ == 3 and later:
                pg_mul(it * 2 - 1, it * 4 - 2)
            if c_ == 4 and later:
                add_squares("pg", it * 2 - 1, sq_n[:, 0, :, :], acc_n)

        for c_ in range(8):
            split("pg", 1, c_)
            if c_ == 0:
                hidden_norm(2)
                link(V.memset(acc_n[:, :, :], 0.0))
                pg_gate(0, (0, 6), 4)
            if c_ == 1:
                pg_mul(0, 0)
            if c_ == 2:
                add_squares("pg", 0, sq_n[:, 0, :, :], acc_n)
            if c_:
                pg_iter(1, c_)
        with dve.Fori(2, 4) as it:
            for c_ in range(8):
                split("pg", it, c_)
                pg_iter(it, c_)
        for c_ in (0, 2, 3):
            pg_iter(4, c_)
        total(3, 4)
        residual(2, ee, V_PLPOST, None)

    ctx.close()


INPUTS = ["x", "p", "positions", "mix_norm_pre", "mix_norm_post", "w_in", "q_norm", "w_uq", "kv_norm", "w_ukv",
          "conv_w", "conv_b", "dt_bias", "a_log", "d_skip", "ssm_norm", "w_attn_o", "w_ssm_o", "w_out",
          "ffn_norm_pre", "ffn_norm_post", "w_gate", "w_up", "w_down",
          "ple_norm_pre", "ple_norm_post", "w_ple_gate", "w_ple"]


def kernel(**inputs):
    import concourse.bacc as bacc
    from concourse.bass_utils import run_bass_kernel_spmd

    nc = bacc.Bacc("TRN2", target_bir_lowering=False, num_devices=1)
    arrays, args = {}, []

    def give(name, a):
        arrays[name] = a
        args.append(nc.dram_tensor(name, a.shape, mybir.dt.from_np(a.dtype), kind="ExternalInput").ap())

    for name in INPUTS:
        a = np.ascontiguousarray(inputs[name])
        while a.ndim > 1 and a.shape[0] == 1:
            a = a[0]
        give(name + "_in", a)
    i = np.arange(P)
    low = (i[:, None] <= i[None, :]).astype(np.float32)
    give("constants", np.concatenate([np.eye(P, dtype=np.float32), low, np.ones((P, P), np.float32)], 1))
    later = np.where(i[None, :] > i[:, None], np.float32(NEG), np.float32(0))
    mask = np.concatenate([later, np.zeros((P, P), np.float32), later], 1)
    rot = np.zeros((P, P), np.float32)
    for half in range(2):
        for f in range(ROPE // 2):
            a, b = 64 * half + f, 64 * half + f + ROPE // 2
            rot[b, a], rot[a, b] = -1.0, 1.0
    freq = (np.float32(THETA) ** (-np.arange(0, ROPE, 2, dtype=np.float32) / np.float32(ROPE))).astype(np.float32)
    eye2 = np.tile(np.eye(P, ROPE, dtype=np.float32), 2)
    give("rotary", np.concatenate([mask, rot, np.tile(freq, 4)[:, None], np.tile(rot[:, 0:ROPE], 2), eye2], 1)
         .astype(np.float32))
    out = nc.dram_tensor("out", (SEQ, D_MODEL), F32, kind="ExternalOutput").ap()
    build(nc, *args, out)
    got = run_bass_kernel_spmd(nc, [arrays], core_ids=[0]).results[0]["out"]
    return got.reshape(1, SEQ, D_MODEL)
```
